# Optimizing a Trainium2 kernel written in Bass

```python
import jax, jax.numpy as jnp
from jax import lax
import numpy as np

D_MODEL = 1024
BATCH = 1
SEQ = 256
DEPTH = 2

CHUNK = 64
N_MEM = 256
NORM_EPS = 1e-6
NEG_BIG = -1e30
GATE_CLIP = 60.0
MIX_WIDTH = D_MODEL
POOL_WIDTH = MIX_WIDTH // 2
POOL_WINDOWS = (2, 4, 8, 16)
POOL_GROUPS = len(POOL_WINDOWS)
POOL_GROUP_DIM = POOL_WIDTH // POOL_GROUPS
REC_WIDTH = MIX_WIDTH - POOL_WIDTH
REC_EXPAND = 128
REC_HEADS = REC_WIDTH // REC_EXPAND
REC_HEAD_DIM = REC_WIDTH // REC_HEADS
ATT_HEADS = 16
ATT_HEAD_DIM = MIX_WIDTH // ATT_HEADS
BAND_CHUNKS = 8
BAND = (BAND_CHUNKS + 1) * CHUNK
REL_CLIP = 256
MEM_HEADS = 4
MEM_HEAD_DIM = D_MODEL // MEM_HEADS
FF_DIM = 4 * D_MODEL
N_EVEN = (DEPTH + 1) // 2
N_ODD = DEPTH // 2


def rmsnorm(x, g):
    xf = x.astype(jnp.float32)
    y = xf * lax.rsqrt(jnp.mean(xf * xf, axis=-1, keepdims=True) + NORM_EPS)
    return y.astype(x.dtype) * g

def causal_multiscale_pool(u):
    S_ = u.shape[1]
    uf = u.astype(jnp.float32)
    cs = jnp.cumsum(uf, axis=1)
    pos = jnp.arange(1, S_ + 1, dtype=jnp.float32)
    outs = []
    for g, w in enumerate(POOL_WINDOWS):
        c = cs[:, :, g]
        lag = jnp.pad(c, ((0, 0), (w, 0), (0, 0)))[:, :S_]
        outs.append((c - lag) / jnp.minimum(pos, w)[:, None])
    mean = jnp.stack(outs, axis=2)
    return (mean - uf).astype(u.dtype)

def hgrn2_chunkwise(q, k, v, logf):
    B_, S_, H, dk = q.shape
    dv = v.shape[-1]
    N = S_ // CHUNK

    def to_chunks(a):
        return a.reshape(B_, N, CHUNK, H, a.shape[-1]).transpose(1, 0, 3, 2, 4)

    causal = jnp.tril(jnp.ones((CHUNK, CHUNK), dtype=bool))[None, None, :, :, None]

    def step(state, inp):
        qc, kc, vc, lc = inp
        b = jnp.cumsum(lc, axis=2)
        o_inter = jnp.einsum('bhtd,bhde->bhte', qc * jnp.exp(b), state)
        diff = b[:, :, :, None, :] - b[:, :, None, :, :]
        decay = jnp.where(causal, jnp.exp(jnp.where(causal, diff, 0.0)), 0.0)
        scores = jnp.einsum('bhtd,bhsd,bhtsd->bhts', qc, kc, decay)
        o = o_inter + jnp.einsum('bhts,bhse->bhte', scores, vc)
        b_last = b[:, :, -1:, :]
        new_state = jnp.exp(b_last[:, :, 0, :])[..., None] * state + jnp.einsum(
            'bhsd,bhse->bhde', kc * jnp.exp(b_last - b), vc)
        return new_state, o

    init = jnp.zeros((B_, H, dk, dv), jnp.float32)
    _, o = lax.scan(step, init, (to_chunks(q), to_chunks(k), to_chunks(v), to_chunks(logf)))
    return o.transpose(1, 0, 3, 2, 4).reshape(B_, S_, H, dv)

def even_mixer(h, w_in, pool_w, pool_scale, lb, out_gain, w_out):
    B_, S_, _ = h.shape
    z = h @ w_in
    cuts = [POOL_WIDTH + r * REC_WIDTH for r in range(4)]
    u, q, fz, i, g = jnp.split(z, cuts, axis=-1)
    pooled = causal_multiscale_pool(u.reshape(B_, S_, POOL_GROUPS, POOL_GROUP_DIM))
    a_out = jnp.einsum('bsgc,gcd->bsgd', pooled, pool_w).reshape(B_, S_, POOL_WIDTH) * pool_scale
    fz32 = jnp.clip(fz.astype(jnp.float32), -GATE_CLIP, GATE_CLIP)
    logf = jax.nn.log_sigmoid(fz32) + jnp.log1p(lb * jnp.exp(-fz32))
    k = (1.0 - lb) * jax.nn.sigmoid(-fz32)
    hs = lambda a: a.reshape(B_, S_, REC_HEADS, -1)
    o = hgrn2_chunkwise(hs(q.astype(jnp.float32)), hs(k), hs(i.astype(jnp.float32)), hs(logf))
    o = rmsnorm(o, out_gain.astype(jnp.float32)) * jax.nn.silu(hs(g.astype(jnp.float32)))
    b_out = o.reshape(B_, S_, REC_WIDTH).astype(h.dtype)
    return jnp.concatenate([a_out.astype(h.dtype), b_out], axis=-1) @ w_out

def chunk_band_attention(q, k, v, rel_bias):
    B_, S_, H, dh = q.shape
    N = S_ // CHUNK
    pad = ((0, 0), (BAND_CHUNKS * CHUNK, 0), (0, 0), (0, 0))
    kp = jnp.pad(k, pad)
    vp = jnp.pad(v, pad)
    t = jnp.arange(CHUNK)[:, None]
    j = jnp.arange(BAND)[None, :]
    rel = BAND_CHUNKS * CHUNK + t - j
    idx = jnp.clip(rel, -REL_CLIP, REL_CLIP) + REL_CLIP
    bias = rel_bias[:, idx].astype(jnp.float32)
    scale = dh ** -0.5

    def per_chunk(n):
        qn = lax.dynamic_slice_in_dim(q, n * CHUNK, CHUNK, axis=1)
        kn = lax.dynamic_slice_in_dim(kp, n * CHUNK, BAND, axis=1)
        vn = lax.dynamic_slice_in_dim(vp, n * CHUNK, BAND, axis=1)
        s = jnp.einsum('bthd,bjhd->bhtj', qn, kn).astype(jnp.float32) * scale + bias
        valid = (n - BAND_CHUNKS) * CHUNK + jnp.arange(BAND) >= 0
        s = jnp.where(valid[None, None, None, :], s, NEG_BIG)
        p = jax.nn.softmax(s, axis=-1).astype(v.dtype)
        return jnp.einsum('bhtj,bjhd->bthd', p, vn)

    out = lax.map(per_chunk, jnp.arange(N))
    return jnp.moveaxis(out, 0, 1).reshape(B_, S_, H, dh)

def odd_mixer(h, w_qkv, rel_bias, w_o):
    B_, S_, _ = h.shape
    qkv = (h @ w_qkv).reshape(B_, S_, 3, ATT_HEADS, ATT_HEAD_DIM)
    o = chunk_band_attention(qkv[:, :, 0], qkv[:, :, 1], qkv[:, :, 2], rel_bias)
    return o.reshape(B_, S_, MIX_WIDTH) @ w_o

def memory_cross_attention(h, mem_n, w_q, w_kv, w_o):
    B_, S_, _ = h.shape
    M = mem_n.shape[1]
    q = (h @ w_q).reshape(B_, S_, MEM_HEADS, MEM_HEAD_DIM)
    kv = (mem_n @ w_kv).reshape(B_, M, 2, MEM_HEADS, MEM_HEAD_DIM)
    s = jnp.einsum('bshd,bmhd->bhsm', q, kv[:, :, 0]).astype(jnp.float32) * MEM_HEAD_DIM ** -0.5
    p = jax.nn.softmax(s, axis=-1).astype(h.dtype)
    o = jnp.einsum('bhsm,bmhd->bshd', p, kv[:, :, 1]).reshape(B_, S_, D_MODEL)
    return o @ w_o

def squared_relu_mlp(h, w1, w2):
    a = jax.nn.relu(h @ w1)
    return (a * a) @ w2

def first_inputs(seed: int = 0) -> dict:
    key = jax.random.key(seed)
    ks = jax.random.split(key, 20)
    f32 = jnp.float32

    def dense(k, shape):
        return jax.random.normal(k, shape, f32) * shape[-2] ** -0.5

    return {
        'x': jax.random.normal(ks[0], (BATCH, SEQ, D_MODEL), f32),
        'mem': jax.random.normal(ks[1], (BATCH, N_MEM, D_MODEL), f32),
        'norm_gains': 1.0 + 0.05 * jax.random.normal(ks[2], (DEPTH, 6, D_MODEL), f32),
        'mem_norm_gain': 1.0 + 0.05 * jax.random.normal(ks[3], (D_MODEL,), f32),
        'w_in_ab': dense(ks[4], (N_EVEN, D_MODEL, POOL_WIDTH + 4 * REC_WIDTH)),
        'pool_w': dense(ks[5], (N_EVEN, POOL_GROUPS, POOL_GROUP_DIM, POOL_GROUP_DIM)),
        'pool_scale': 1.0 + 0.1 * jax.random.normal(ks[6], (N_EVEN, POOL_WIDTH), f32),
        'rec_lb_logits': 0.1 * jax.random.normal(ks[7], (N_EVEN, REC_WIDTH), f32),
        'rec_out_gain': 1.0 + 0.05 * jax.random.normal(ks[8], (N_EVEN, REC_HEAD_DIM), f32),
        'w_out_ab': dense(ks[9], (N_EVEN, MIX_WIDTH, D_MODEL)),
        'w_qkv': dense(ks[10], (N_ODD, D_MODEL, 3 * MIX_WIDTH)),
        'rel_bias': 0.1 * jax.random.normal(ks[11], (N_ODD, ATT_HEADS, 2 * REL_CLIP + 1), f32),
        'w_o_att': dense(ks[12], (N_ODD, MIX_WIDTH, D_MODEL)),
        'w_mem_q': dense(ks[13], (DEPTH, D_MODEL, D_MODEL)),
        'w_mem_kv': dense(ks[14], (DEPTH, D_MODEL, 2 * D_MODEL)),
        'w_mem_o': dense(ks[15], (DEPTH, D_MODEL, D_MODEL)),
        'w_ff1': dense(ks[16], (DEPTH, D_MODEL, FF_DIM)),
        'w_ff2': dense(ks[17], (DEPTH, FF_DIM, D_MODEL)),
    }

def first_block(x, mem, norm_gains, mem_norm_gain, w_in_ab, pool_w, pool_scale, rec_lb_logits,
              rec_out_gain, w_out_ab, w_qkv, rel_bias, w_o_att, w_mem_q, w_mem_kv, w_mem_o,
              w_ff1, w_ff2):
    lb_p = jax.nn.softmax(rec_lb_logits.astype(jnp.float32), axis=0)
    lbs = jnp.clip(jnp.cumsum(lb_p, axis=0) - lb_p[0], 0.0, 1.0)
    mem_n = rmsnorm(mem, mem_norm_gain)
    for l in range(DEPTH):
        g = norm_gains[l]
        h = rmsnorm(x, g[0])
        if l % 2 == 0:
            e = l // 2
            y = even_mixer(h, w_in_ab[e], pool_w[e], pool_scale[e], lbs[e], rec_out_gain[e],
                           w_out_ab[e])
        else:
            o = l // 2
            y = odd_mixer(h, w_qkv[o], rel_bias[o], w_o_att[o])
        x = x + rmsnorm(y, g[1])
        h = rmsnorm(x, g[2])
        x = x + rmsnorm(memory_cross_attention(h, mem_n, w_mem_q[l], w_mem_kv[l], w_mem_o[l]), g[3])
        h = rmsnorm(x, g[4])
        x = x + rmsnorm(squared_relu_mlp(h, w_ff1[l], w_ff2[l]), g[5])
    return x


N_A_LAYERS = DEPTH // 2
N_B_LAYERS = DEPTH - N_A_LAYERS
HEAD_DIM = 64
SB_HEADS = D_MODEL // HEAD_DIM
SWA_Q_HEADS = D_MODEL // HEAD_DIM
SWA_KV_HEADS = 4
SWA_GROUP = SWA_Q_HEADS // SWA_KV_HEADS
WINDOW = 128
Q_BLOCK = 128
D_FF = 2816
ROPE_THETA = 10000.0
RMS_EPS = 1e-6
FFN_RES_SCALE = 0.5


def rms_norm(x, g):
    xf = x.astype(jnp.float32)
    y = xf * lax.rsqrt(jnp.mean(xf * xf, axis=-1, keepdims=True) + RMS_EPS)
    return (y * g.astype(jnp.float32)).astype(x.dtype)

def swiglu(x, w_in, w_out):
    gate, up = jnp.split(x @ w_in, 2, axis=-1)
    return (jax.nn.silu(gate) * up) @ w_out

def rotary(x, pos):
    half = HEAD_DIM // 2
    inv_freq = ROPE_THETA ** (-jnp.arange(half, dtype=jnp.float32) / half)
    ang = pos.astype(jnp.float32)[:, None] * inv_freq[None, :]
    cos = jnp.cos(ang)[None, :, None, :]
    sin = jnp.sin(ang)[None, :, None, :]
    xf = x.astype(jnp.float32)
    x1, x2 = xf[..., :half], xf[..., half:]
    return jnp.concatenate([x1 * cos - x2 * sin, x2 * cos + x1 * sin], axis=-1).astype(x.dtype)

def stick_breaking_attention(q, k, v):
    B, S, H, Dh = q.shape
    nb = S // Q_BLOCK
    scale = Dh ** -0.5
    key_pos = jnp.arange(S)
    qb = q.reshape(B, nb, Q_BLOCK, H, Dh).transpose(1, 0, 2, 3, 4)

    def block(args):
        qi, i = args
        z = jnp.einsum('bqhd,bshd->bhqs', qi, k).astype(jnp.float32) * scale
        q_pos = i * Q_BLOCK + jnp.arange(Q_BLOCK)
        strict = key_pos[None, :] < q_pos[:, None]
        log_beta = jax.nn.log_sigmoid(z)
        log_1m_beta = jnp.where(strict, log_beta - z, 0.0)
        suffix = lax.cumsum(log_1m_beta, axis=3, reverse=True) - log_1m_beta
        w = jnp.where(strict, jnp.exp(log_beta + suffix), 0.0)
        return jnp.einsum('bhqs,bshd->bqhd', w.astype(v.dtype), v)

    out = lax.map(block, (qb, jnp.arange(nb)))
    return out.transpose(1, 0, 2, 3, 4).reshape(B, S, H, Dh)

def sliding_window_sink_attention(q, k, v, sinks):
    B, S, Hq, Dh = q.shape
    nb = S // WINDOW
    qb = q.reshape(B, nb, WINDOW, SWA_KV_HEADS, SWA_GROUP, Dh)

    def band(t):
        tb = t.reshape(B, nb, WINDOW, SWA_KV_HEADS, Dh)
        prev = jnp.pad(tb[:, :-1], ((0, 0), (1, 0), (0, 0), (0, 0), (0, 0)))
        return jnp.concatenate([prev, tb], axis=2)

    kb, vb = band(k), band(v)
    s = jnp.einsum('bnqhgd,bnkhd->bnhgqk', qb, kb).astype(jnp.float32) * (Dh ** -0.5)
    qi = jnp.arange(WINDOW)[:, None]
    ki = jnp.arange(2 * WINDOW)[None, :]
    diff = qi + WINDOW - ki
    in_window = (diff >= 0) & (diff < WINDOW)
    blk = jnp.arange(nb)[:, None, None]
    valid = in_window[None] & ((blk > 0) | (ki[None] >= WINDOW))
    s = jnp.where(valid[None, :, None, None], s, -jnp.inf)
    sink = jnp.broadcast_to(
        sinks.astype(jnp.float32).reshape(SWA_KV_HEADS, SWA_GROUP)[None, None, :, :, None, None],
        s.shape[:-1] + (1,))
    p = jax.nn.softmax(jnp.concatenate([s, sink], axis=-1), axis=-1)[..., :-1]
    out = jnp.einsum('bnhgqk,bnkhd->bnqhgd', p.astype(v.dtype), vb)
    return out.reshape(B, S, Hq, Dh)

def second_inputs(seed: int = 0) -> dict:
    key = jax.random.key(seed)
    ks = jax.random.split(key, 20)
    f32 = jnp.float32

    def w(k, shape, fan_in):
        return jax.random.normal(k, shape, f32) * (fan_in ** -0.5)

    def gain(k, shape):
        return 1.0 + 0.02 * jax.random.normal(k, shape, f32)

    return {
        "x": jax.random.normal(ks[0], (BATCH, SEQ, D_MODEL), f32),
        "ffn1_norm": gain(ks[1], (DEPTH, D_MODEL)),
        "ffn1_w_in": w(ks[2], (DEPTH, D_MODEL, 2 * D_FF), D_MODEL),
        "ffn1_w_out": w(ks[3], (DEPTH, D_FF, D_MODEL), D_FF),
        "mix_norm": gain(ks[4], (DEPTH, D_MODEL)),
        "ffn2_norm": gain(ks[5], (DEPTH, D_MODEL)),
        "ffn2_w_in": w(ks[6], (DEPTH, D_MODEL, 2 * D_FF), D_MODEL),
        "ffn2_w_out": w(ks[7], (DEPTH, D_FF, D_MODEL), D_FF),
        "sb_w_qkv": w(ks[8], (N_A_LAYERS, D_MODEL, 3 * SB_HEADS * HEAD_DIM), D_MODEL),
        "sb_w_o": w(ks[9], (N_A_LAYERS, SB_HEADS * HEAD_DIM, D_MODEL), SB_HEADS * HEAD_DIM),
        "kv_norm": gain(ks[10], (D_MODEL,)),
        "kv_w": w(ks[11], (D_MODEL, 2 * SWA_KV_HEADS * HEAD_DIM), D_MODEL),
        "swa_w_q": w(ks[12], (N_B_LAYERS, D_MODEL, SWA_Q_HEADS * HEAD_DIM), D_MODEL),
        "swa_sinks": 0.5 * jax.random.normal(ks[13], (N_B_LAYERS, SWA_Q_HEADS), f32),
        "swa_w_o": w(ks[14], (N_B_LAYERS, SWA_Q_HEADS * HEAD_DIM, D_MODEL), SWA_Q_HEADS * HEAD_DIM),
        "final_norm": gain(ks[15], (D_MODEL,)),
    }

def second_block(x, ffn1_norm, ffn1_w_in, ffn1_w_out, mix_norm, ffn2_norm, ffn2_w_in, ffn2_w_out,
              sb_w_qkv, sb_w_o, kv_norm, kv_w, swa_w_q, swa_sinks, swa_w_o, final_norm):
    B, S, D = x.shape
    pos = jnp.arange(S)
    h = x
    k_shared = None
    v_shared = None
    for layer in range(DEPTH):
        h = h + FFN_RES_SCALE * swiglu(rms_norm(h, ffn1_norm[layer]), ffn1_w_in[layer], ffn1_w_out[layer])
        hn = rms_norm(h, mix_norm[layer])
        if layer < N_A_LAYERS:
            qkv = (hn @ sb_w_qkv[layer]).reshape(B, S, 3, SB_HEADS, HEAD_DIM)
            o = stick_breaking_attention(qkv[:, :, 0], qkv[:, :, 1], qkv[:, :, 2])
            h = h + o.reshape(B, S, SB_HEADS * HEAD_DIM) @ sb_w_o[layer]
        else:
            j = layer - N_A_LAYERS
            q = rotary((hn @ swa_w_q[j]).reshape(B, S, SWA_Q_HEADS, HEAD_DIM), pos)
            o = sliding_window_sink_attention(q, k_shared, v_shared, swa_sinks[j])
            h = h + o.reshape(B, S, SWA_Q_HEADS * HEAD_DIM) @ swa_w_o[j]
        h = h + FFN_RES_SCALE * swiglu(rms_norm(h, ffn2_norm[layer]), ffn2_w_in[layer], ffn2_w_out[layer])
        if layer == N_A_LAYERS - 1:
            kv = (rms_norm(h, kv_norm) @ kv_w).reshape(B, S, 2, SWA_KV_HEADS, HEAD_DIM)
            k_shared = rotary(kv[:, :, 0], pos)
            v_shared = kv[:, :, 1]
    return rms_norm(h, final_norm)


def setup_inputs(seed=0):
    out = dict(first_inputs(seed))
    for name, value in second_inputs(seed + 1).items():
        if name != "x":
            out[name + "_2"] = value
    return out


def reference(
    x, mem, norm_gains, mem_norm_gain, w_in_ab, pool_w, pool_scale, rec_lb_logits, rec_out_gain,
    w_out_ab, w_qkv, rel_bias, w_o_att, w_mem_q, w_mem_kv, w_mem_o, w_ff1, w_ff2, ffn1_norm_2,
    ffn1_w_in_2, ffn1_w_out_2, mix_norm_2, ffn2_norm_2, ffn2_w_in_2, ffn2_w_out_2, sb_w_qkv_2,
    sb_w_o_2, kv_norm_2, kv_w_2, swa_w_q_2, swa_sinks_2, swa_w_o_2, final_norm_2,
):
    x = first_block(
        x, mem, norm_gains, mem_norm_gain, w_in_ab, pool_w, pool_scale, rec_lb_logits,
        rec_out_gain, w_out_ab, w_qkv, rel_bias, w_o_att, w_mem_q, w_mem_kv, w_mem_o, w_ff1,
        w_ff2,
    )
    return second_block(
        x, ffn1_norm_2, ffn1_w_in_2, ffn1_w_out_2, mix_norm_2, ffn2_norm_2, ffn2_w_in_2,
        ffn2_w_out_2, sb_w_qkv_2, sb_w_o_2, kv_norm_2, kv_w_2, swa_w_q_2, swa_sinks_2,
        swa_w_o_2, final_norm_2,
    )


_drawn_inputs = setup_inputs


def setup_inputs(seed=0):
    import zlib

    import numpy as np

    out = dict(_drawn_inputs(seed))
    spreads = {}
    factors = {'rec_out_gain': 2.774,
     'rel_bias': 4.163,
     'ffn1_norm_2': 8.0,
     'mix_norm_2': 8.0,
     'ffn2_norm_2': 8.0,
     'kv_norm_2': 8.0,
     'swa_sinks_2': 200.0,
     'final_norm_2': 23.749}
    for name, (base, spread) in spreads.items():
        noise = np.random.default_rng([zlib.crc32(name.encode()), seed]).standard_normal(out[name].shape)
        drawn = base * np.exp(spread * noise) if base else spread * noise
        out[name] = __import__('jax').numpy.asarray(drawn.astype(out[name].dtype))
    for name, factor in factors.items():
        out[name] = (out[name] * factor).astype(out[name].dtype)
    return out
```

```python
from contextlib import ExitStack

import numpy as np

import concourse.bass as bass
from concourse import mybir

P = 128
S = 256
TB = S // P
D = 1024
KT = D // P
CH = 256
RAW = 3
RING = 3
AHEAD = RING - 1
EPS = 1e-6
NEG = -1e30
LOWEST = -3e38
REL = 256
FF = 4096
DFF = 2816
LEVELS = (64, 32, 16, 8, 4, 2, 1)
POOL_WINDOWS = (2, 4, 8, 16)
GATE_CLIP = 60.0
N_NORMS = 24


class Counts:

    def __init__(self, norm, xn, turned, x, chunk, copied, hid, hid_hi, up, head, ctx, rot):
        self.norm, self.xn, self.turned, self.x, self.chunk, self.copied = norm, xn, turned, x, chunk, copied
        self.hid, self.hid_hi, self.up, self.head, self.ctx, self.rot = hid, hid_hi, up, head, ctx, rot


def constants():
    i = np.arange(P)
    t = {}
    t["ident"] = np.eye(P)
    t["after"] = (i[:, None] > i[None, :])
    t["upto"] = (i[:, None] <= i[None, :])
    span, pair = [], []
    for m in LEVELS:
        half = (i // m) % 2
        mid = (i // (2 * m)) * 2 * m + m - 1
        tau, tok = i[:, None], i[None, :]
        right = (half[None, :] == 1) & (tau > mid[None, :]) & (tau <= tok)
        left = (half[None, :] == 0) & (tau > tok) & (tau <= mid[None, :])
        span.append(right | left)
        same = (i[:, None] // (2 * m)) == (i[None, :] // (2 * m))
        pair.append(same & (half[:, None] == 0) & (half[None, :] == 1))
    t["span"] = np.concatenate(span, 1)
    t["pair"] = np.concatenate(pair, 1)
    tok = np.arange(S)
    pool = []
    for w in POOL_WINDOWS:
        for b in range(TB):
            tau = b * P + i[:, None]
            inside = (tau <= tok[None, :]) & (tau > tok[None, :] - w)
            count = np.minimum(tok + 1, w).astype(np.float32)[None, :]
            pool.append(inside / count - (tau == tok[None, :]))
    t["pool"] = np.concatenate(pool, 1)
    q = tok.reshape(TB, P)
    band, swa = [], []
    for b in range(TB):
        qq = q[b][:, None]
        kk = tok[None, :]
        seen = slice(0, (b + 1) * P)
        band.append(np.where(kk // 64 <= qq // 64, 0.0, NEG)[:, seen])
        swa.append(np.where((qq - kk >= 0) & (qq - kk < 128), 0.0, NEG)[:, seen])
    t["band"] = np.concatenate(band, 1)
    t["swa"] = np.concatenate(swa, 1)
    t["strict"] = (i[:, None] < i[None, :])
    half = 32
    freq = np.float32(10000.0) ** (-np.arange(half, dtype=np.float32) / np.float32(half))
    ang = tok.astype(np.float32)[None, :] * freq[:, None].astype(np.float32)
    t["cos"] = np.tile(np.cos(ang), (4, 1))
    t["sin"] = np.tile(np.sin(ang), (4, 1))
    turn = np.zeros((P, P))
    for d in range(P):
        if d % 64 < half:
            turn[d + half, d] = -1.0
        else:
            turn[d - half, d] = 1.0
    t["turn"] = turn
    t["low"] = np.concatenate([np.eye(64), np.zeros((64, 64))], 0) @ np.concatenate([np.eye(64), np.eye(64)], 1)
    t["high"] = np.concatenate([np.zeros((64, 64)), np.eye(64)], 0) @ np.concatenate([np.eye(64), np.eye(64)], 1)
    t["flip"] = 8.0 * np.eye(P)[::-1]
    t["ones"] = np.ones((P, P))
    return {k: np.ascontiguousarray(v, dtype=np.float32) for k, v in t.items()}


def build(nc, a, out):
    f32 = mybir.dt.float32
    f32r = mybir.dt.float32r
    bf16 = mybir.dt.bfloat16
    i32 = mybir.dt.int32
    ACT = mybir.ActivationFunctionType
    ALU = mybir.AluOpType
    X = mybir.AxisListType.X
    ctx = ExitStack()

    def sb(name, shape, dt=f32):
        return ctx.enter_context(nc.sbuf_tensor(name, shape, dt))

    def sem(name):
        return ctx.enter_context(nc.semaphore(name))

    with ctx:
        raw = sb("raw", [P, RAW, 2048])
        w_hi = sb("w_hi", [P, RING, 2048], f32r)
        w_lo = sb("w_lo", [P, RING, 2048], f32r)
        x = sb("x", [P, TB, D])
        xn = sb("xn", [P, TB, D])
        at_h = sb("at_h", [P, KT, S], f32r)
        at_l = sb("at_l", [P, KT, S], f32r)
        mem_h = sb("mem_h", [P, KT, S], f32r)
        mem_l = sb("mem_l", [P, KT, S], f32r)
        hid_h = sb("hid_h", [P, 3, 2 * S], f32r)
        hid_l = sb("hid_l", [P, 3, 2 * S], f32r)
        gain = sb("gain", [P, 2, D])
        ident = sb("ident", [P, P])
        zeros = sb("zeros", [P, 512], bf16)
        stat = sb("stat", [P, 8, 2 * N_NORMS])
        eps = sb("eps", [P, 1])
        arena = sb("arena", [P, 15872])
        Y = ctx.enter_context(nc.psum_tensor("Y", [P, 4, 512], f32))
        C = ctx.enter_context(nc.psum_tensor("C", [P, 4, 512], f32))
        used = [0]

        def room(cols, start=None):
            at = used[0] if start is None else start
            used[0] = at + cols
            assert used[0] <= 15872
            return arena[:, at:at + cols]

        def tiles(ap, n):
            return ap.rearrange("p (a b) -> p a b", a=n)

        mem_x = tiles(room(TB * D, 0), TB)
        room(0, 0)
        u_t, f_t, v_t, g_t = (tiles(room(TB * 512), TB) for _ in range(4))
        q_d, k_d = (tiles(room(4 * S), 4) for _ in range(2))
        fall = [room(4 * S) for _ in range(2)]
        both = [tiles(room(4 * S), 4) for _ in range(2)]
        scores = room(3 * 4 * P)
        score = [tiles(scores[:, i * 4 * P:(i + 1) * 4 * P], 4) for i in range(3)]
        span_c = room(len(LEVELS) * P)
        pair_c = room(len(LEVELS) * P)
        after_c = room(P)
        upto_c = room(P)
        lb = room(512)
        not_lb = room(512)
        og = room(P)
        pscale = room(4)
        h_stat = tiles(room(8 * 8), 8)
        pool_w = tiles(room(4 * P), 4)
        flat = "p a b -> p (a b)"
        pool_c = [both[0].rearrange(flat), fall[0]]
        pooled = both[1]
        exp_f = k_d.rearrange(flat)
        soft_f = fall[1]
        key = scores[:, 0:TB * 512]
        room(0, 0)
        qT, kT = (tiles(room(8 * S), 8) for _ in range(2))
        vt = tiles(room(TB * D), TB)
        SEEN = 3 * P
        sc = [room(2 * S) for _ in range(2)]
        pr = [room(2 * S) for _ in range(3)]
        pT = [room(2 * S) for _ in range(3)]
        bias = [room(2 * S) for _ in range(2)]
        mask = room(SEEN)
        a_stat = tiles(room(5 * 32), 5)
        sinks = room(32)
        rope = tiles(room(2 * S), 2)
        turn_c = room(P)
        low_c, high_c, after_s, ones_s = (room(P) for _ in range(4))
        flip_c = room(P)
        rot = [room(2 * S) for _ in range(2)]
        kdup = tiles(room(4 * S), 4)
        relu = sc + bias[:1]
        full = pr

        loaded = [sem(f"loaded{i}") for i in range(RAW)]
        hi_split = sem("hi_split")
        lo_split = sem("lo_split")
        chunk_done = sem("chunk_done")
        cols_copied = sem("cols_copied")
        up_used = sem("up_used")
        guessed = sem("guessed")
        x_ready = sem("x_ready")
        xn_ready = sem("xn_ready")
        xt_ready = sem("xt_ready")
        at_hi = sem("at_hi")
        at_lo = sem("at_lo")
        gains_in = [sem(f"gains_in{i}") for i in range(2)]
        hid_hi = sem("hid_hi")
        hid_lo = sem("hid_lo")
        act_seq = sem("act_seq")
        dve_seq = sem("dve_seq")
        tokens_in, mem_in, ident_in = sem("tokens_in"), sem("mem_in"), sem("ident_in")
        setup = sem("setup")
        out_done = sem("out_done")
        even_in, pool_in = sem("even_in"), sem("pool_in")
        band_in, stick_in, swa_in = sem("band_in"), sem("stick_in"), sem("swa_in")
        bias_in = [sem(f"bias_in{i}") for i in range(2)]
        lb_shifted, lb_exp = sem("lb_shifted"), sem("lb_exp")
        clipped, gates_exp, lb_scaled = sem("clipped"), sem("gates_exp"), sem("lb_scaled")
        gates_ln, keys_ready, decays_ready = sem("gates_ln"), sem("keys_ready"), sem("decays_ready")
        keys_turned, keys_copied = sem("keys_turned"), sem("keys_copied")
        pool_ready, pool_copied = sem("pool_ready"), sem("pool_copied")
        mix_ready, mix_hi, mix_lo = sem("mix_ready"), sem("mix_hi"), sem("mix_lo")
        level_sum, level_exp, level_both = sem("level_sum"), sem("level_exp"), sem("level_both")
        level_score, level_used = sem("level_score"), sem("level_used")
        rec_ready, rec_squared, rec_meaned = sem("rec_ready"), sem("rec_squared"), sem("rec_meaned")
        rec_guessed, rec_normed, rec_turned = sem("rec_guessed"), sem("rec_normed"), sem("rec_turned")
        rec_hi, rec_lo = sem("rec_hi"), sem("rec_lo")
        scores_ready = sem("scores_ready")
        scores_scaled = sem("scores_scaled")
        scores_max = sem("scores_max")
        probs_ready = sem("probs_ready")
        probs_scaled = sem("probs_scaled")
        probs_turned = sem("probs_turned")
        probs_copied = sem("probs_copied")
        probs_used = sem("probs_used")
        sink_ready = sem("sink_ready")
        ctx_hi, ctx_lo = sem("ctx_hi"), sem("ctx_lo")
        turned, rotated = sem("turned"), sem("rotated")
        kdup_ready, kdup_copied = sem("kdup_ready"), sem("kdup_copied")
        z_ready = sem("z_ready")
        soft_ready = sem("soft_ready")
        keep_ready = sem("keep_ready")
        keep_masked = sem("keep_masked")
        suffix_ready = sem("suffix_ready")
        suffix_added = sem("suffix_added")
        weights_ready = sem("weights_ready")
        weights_masked = sem("weights_masked")
        weights_used = sem("weights_used")

        def weight(name, l):
            return a[name] if l is None else a[name][l]

        def col(name, l, c, off=0):
            first = c * CH + off
            return weight(name, l).rearrange("(k p) n -> p k n", p=P)[:, :, bass.ds(first, CH)]

        def row(name, l, r, off=0):
            return weight(name, l)[bass.ds(r * CH + off, CH), :].rearrange("(k p) n -> p k n", p=P)

        even_cols = [("w_in_ab", 0, c, kind, "at") for c, kind in enumerate("NNTTNNNNNN")]
        qkv_cols = [("w_qkv", 0, c, "TTN"[c // 4], "at") for c in range(12)]
        stick_cols = [("sb_w_qkv_2", 0, c, "TTN"[c // 4], "at") for c in range(12)]
        kv_cols = [("kv_w_2", None, 0, "T", "at"), ("kv_w_2", None, 1, "N", "at")]
        q_cols = [("swa_w_q_2", 0, c, "T", "at") for c in range(4)]

        def mem_cols(l):
            return ([("w_mem_q", l, c, "T", "at") for c in range(4)]
                    + [("w_mem_kv", l, c, "T", "mem") for c in range(4)]
                    + [("w_mem_kv", l, 4 + c, "N", "mem") for c in range(4)])

        def halves(t, c):
            return t[:, 2 * c:2 * c + 2, :]

        def wide(t, c):
            return t[:, :, c * CH:(c + 1) * CH]

        even_to = [wide(u_t, 0), wide(u_t, 1), halves(q_d, 0), halves(q_d, 1), wide(f_t, 0), wide(f_t, 1),
                   wide(v_t, 0), wide(v_t, 1), wide(g_t, 0), wide(g_t, 1)]
        qkv_to = [halves(qT, c) for c in range(4)] + [halves(kT, c) for c in range(4)] + [wide(vt, c) for c in range(4)]
        kv_to = [halves(kT, 0), wide(vt, 0)]
        q_to = [halves(qT, c) for c in range(4)]

        ng = a["norm_gains"]
        gain_rows = [a["mem_norm_gain"], ng[0, 0], *(ng[0, i] for i in range(1, 6)), *(ng[1, i] for i in range(6)),
                     a["ffn1_norm_2"][0], a["mix_norm_2"][0], a["ffn2_norm_2"][0], a["kv_norm_2"],
                     a["ffn1_norm_2"][1], a["mix_norm_2"][1], a["ffn2_norm_2"][1], a["final_norm_2"]]

        net = [("norm", "mem"), ("norm", "at"), ("cols", even_cols, even_to), ("even",), ("rows", "w_out_ab", 0),
               ("post",), ("norm", "at")]
        for l in range(2):
            if l == 1:
                net += [("cols", qkv_cols, qkv_to), ("softmax", "band", 16), ("rows", "w_o_att", 0),
                        ("post",), ("norm", "at")]
            net += [("cols", mem_cols(l), qkv_to), ("softmax", "mem", 4), ("rows", "w_mem_o", l),
                    ("post",), ("norm", "at"), ("relu_ff", l), ("post",), ("norm", "at")]
        for l in range(2):
            net += [("swiglu", "ffn1", l), ("add", 0.5), ("norm", "at")]
            if l == 0:
                net += [("cols", stick_cols, qkv_to), ("stick",), ("rows", "sb_w_o_2", 0)]
            else:
                net += [("cols", q_cols, q_to), ("rope", "q", 4), ("softmax", "swa", 16), ("rows", "swa_w_o_2", 0)]
            net += [("add", 1.0), ("norm", "at"), ("swiglu", "ffn2", l), ("add", 0.5)]
            if l == 0:
                net += [("norm", "at"), ("cols", kv_cols, kv_to), ("rope", "k", 1), ("norm", "at")]
        net += [("norm", "out")]

        N_REL, N_GLU = FF // CH, DFF // CH

        def counts(s):
            if s[0] == "norm":
                return dict(norm=1, xn=2, turned=4 * (s[1] != "out"))
            if s[0] == "post":
                return dict(norm=1, x=2)
            if s[0] == "add":
                return dict(x=2)
            if s[0] == "cols":
                return dict(chunk=len(s[1]), copied=len(s[1]))
            if s[0] == "rows":
                return dict(chunk=4)
            if s[0] == "relu_ff":
                return dict(chunk=2 * N_REL, copied=N_REL, hid=N_REL, hid_hi=N_REL)
            if s[0] == "swiglu":
                return dict(chunk=3 * N_GLU, copied=N_GLU, up=N_GLU, hid=N_GLU)
            if s[0] == "softmax":
                return dict(head=s[2], ctx=4 if s[1] == "mem" else 8)
            if s[0] == "stick":
                return dict(ctx=8)
            if s[0] == "rope":
                return dict(rot=s[2])
            return {}

        before, so_far = [], dict(norm=0, xn=0, turned=0, x=0, chunk=0, copied=0, hid=0,
                                  hid_hi=0, up=0, head=0, ctx=0, rot=0)
        for s in net:
            before.append((s, Counts(**so_far)))
            for k, v in counts(s).items():
                so_far[k] += v
        N_CHUNKS = so_far["chunk"]

        def glu_turns(n):
            return (N_GLU - 1) // 2 - (n + 3 * N_GLU == N_CHUNKS)

        gain_done = [(xn_ready, at.xn + TB) if s[0] == "norm" else (x_ready, at.x + TB)
                     for s, at in before if s[0] in ("norm", "post")]

        def rows_of(kind):
            return ((0, S), (S, 2 * S)) if kind == "mem" else ((0, P), (P, SEEN))

        block = ctx.enter_context(nc.Block())

        @block.sync
        def _(sp):
            def load(src, slot, at, first=False):
                if not first:
                    sp.wait_ge(lo_split, at - RAW + 1)
                sp.dma_start(raw[:, slot, :].rearrange("p (k n) -> p k n", k=src.shape[1]), src) \
                    .then_inc(loaded[slot], 16)

            sp.dma_start(mem_x, a["mem"][0].rearrange("(b p) d -> p b d", p=P)).then_inc(mem_in, 16)
            sp.dma_start(x[:], a["x"][0].rearrange("(b p) d -> p b d", p=P)).then_inc(tokens_in, 16)
            for s, at in before:
                n = at.chunk
                if s[0] == "cols":
                    for i, (name, l, c, _, _) in enumerate(s[1]):
                        load(col(name, l, c), (n + i) % RAW, n + i, n + i < RAW)
                elif s[0] == "rows":
                    for r in range(4):
                        load(row(s[1], s[2], r), (n + r) % RAW, n + r)
                elif s[0] == "relu_ff":
                    l, end = s[1], n + 2 * N_REL - 1
                    load(col("w_ff1", l, 0), n % RAW, n)
                    with nc.sync.Fori(0, (N_REL - 1) // 3) as t:
                        for j in range(3):
                            up, down = n + 1 + 2 * j, n + 2 + 2 * j
                            load(col("w_ff1", l, j + 1, t * (3 * CH)), up % RAW, t * 6 + up)
                            load(row("w_ff2", l, j, t * (3 * CH)), down % RAW, t * 6 + down)
                    load(row("w_ff2", l, N_REL - 1), end % RAW, end)
                elif s[0] == "swiglu":
                    wi, wo, l, end = s[1] + "_w_in_2", s[1] + "_w_out_2", s[2], n + 3 * N_GLU - 1
                    load(col(wi, l, 0), n % RAW, n)
                    load(col(wi, l, N_GLU), (n + 1) % RAW, n + 1)
                    with nc.sync.Fori(0, (N_GLU - 1) // 2) as t:
                        for j in range(2):
                            gate = n + 2 + 3 * j
                            load(col(wi, l, j + 1, t * (2 * CH)), gate % RAW, t * 6 + gate)
                            load(col(wi, l, N_GLU + j + 1, t * (2 * CH)), (gate + 1) % RAW, t * 6 + (gate + 1))
                            load(row(wo, l, j, t * (2 * CH)), (gate + 2) % RAW, t * 6 + (gate + 2))
                    load(row(wo, l, N_GLU - 1), end % RAW, end)
                elif s == ("norm", "out"):
                    for b in range(TB):
                        sp.wait_ge(xn_ready, at.xn + b + 1)
                        sp.dma_start(out[0, b * P:(b + 1) * P, :], xn[:, b, :]).then_inc(out_done, 16)
            sp.wait_ge(out_done, 16 * TB)

        @block.gpsimd
        def _(pool):
            nc.gpsimd.memset(eps[:], EPS)
            nc.gpsimd.memset(zeros[:], 0.0).then_inc(setup, 1)
            pool.dma_start(ident[:], a["ident"]).then_inc(ident_in, 16)
            for s, at in before:
                if s[0] in ("norm", "post"):
                    i = at.norm
                    if i >= 2:
                        pool.wait_ge(*gain_done[i - 2])
                    pool.dma_start(gain[:, i % 2, :], gain_rows[i].partition_broadcast(P)).then_inc(gains_in[i % 2], 16)
                elif s[0] == "cols" and s[1] is even_cols:
                    for to, src in ((span_c, a["span"]), (pair_c, a["pair"]), (after_c, a["after"]), (upto_c, a["upto"]),
                                    (lb, a["rec_lb_logits"][0].partition_broadcast(P)),
                                    (og, a["rec_out_gain"][0].partition_broadcast(P)),
                                    (pool_w, a["pool_w"][0].rearrange("g c d -> c g d")),
                                    (pscale, a["pool_scale_by_group"])):
                        pool.dma_start(to, src).then_inc(even_in, 16)
                    for i in range(2):
                        pool.dma_start(pool_c[i], a["pool"][:, i * 4 * S:(i + 1) * 4 * S]).then_inc(pool_in, 16)
                elif s[0] == "cols" and s[1] is qkv_cols:
                    pool.wait_ge(x_ready, at.x)
                    pool.dma_start(mask, a["band"]).then_inc(band_in, 16)
                    pool.dma_start(flip_c, a["flip"]).then_inc(band_in, 16)
                elif s[0] == "cols" and s[1] is stick_cols:
                    pool.wait_ge(x_ready, at.x)
                    for to, src in ((mask[:, 0:P], a["strict"]), (after_s, a["after"]), (ones_s, a["ones"])):
                        pool.dma_start(to, src).then_inc(stick_in, 16)
                elif s[0] == "cols" and s[1] is kv_cols:
                    pool.wait_ge(x_ready, at.x)
                    for to, src in ((rope[:, 0, :], a["cos"]), (rope[:, 1, :], a["sin"]), (turn_c, a["turn"]),
                                    (low_c, a["low"]), (high_c, a["high"]), (mask, a["swa"]),
                                    (sinks[:, 0:16], a["swa_sinks_2"][0].partition_broadcast(P))):
                        pool.dma_start(to, src).then_inc(swa_in, 16)
                elif s[0] == "softmax" and s[1] == "band":
                    table = a["rel_reversed"]
                    for h in range(16):
                        if h >= 2:
                            pool.wait_ge(scores_ready, at.head + h - 1)
                        for b in range(TB):
                            src = bass.AP(table.tensor, h * (2 * REL + 1) + REL - b * P - (P - 1), [[1, P], [1, (b + 1) * P]])
                            pool.dma_start(bias[h % 2][:, b * P:b * P + (b + 1) * P], src).then_inc(bias_in[h % 2], 16)
                elif s[0] == "stick":
                    pool.wait_ge(stick_in, 48)
                    strict = mask[:, None, 0:P].broadcast_to([P, 2, P])
                    for i in range(16 + 2):
                        if i < 16:
                            pool.wait_ge(keep_ready, i + 1)
                            own = tiles(pr[i % 2][:, 0:SEEN], 3)[:, 0:3:2, :]
                            nc.gpsimd.tensor_tensor(own, own, strict, ALU.mult).then_inc(keep_masked, 1)
                        if i >= 2:
                            pool.wait_ge(weights_ready, i - 1)
                            own = tiles(pT[(i - 2) % 3][:, 0:SEEN], 3)[:, 0:3:2, :]
                            nc.gpsimd.tensor_tensor(own, own, strict, ALU.mult).then_inc(weights_masked, 1)

        @block.scalar
        def _(act):
            seq = [0]

            def again(ins):
                seq[0] += 1
                ins.then_inc(act_seq, 1)
                act.wait_ge(act_seq, seq[0])

            def exp_and_ln():
                nc.scalar.preload_act_table_set("natural_log_exp_and_others")

            def hi(n, t=None):
                if n >= N_CHUNKS:
                    return
                step = (lambda k, v: v) if t is None else (lambda k, v: t * k + v)
                act.wait_ge(loaded[n % RAW], step(6 // RAW * 16, 16 * (n // RAW + 1)))
                if n >= RING:
                    act.wait_ge(chunk_done, step(6, n - RING + 1))
                nc.scalar.activation(w_hi[:, n % RING, :], raw[:, n % RAW, :], ACT.Copy).then_inc(hi_split, 1)

            def guess(src, b, at):
                j = 2 * at.norm + b
                again(nc.scalar.activation(xn[:, b, :], src, ACT.Square, accum_out=stat[:, 0, j:j + 1]))
                again(nc.scalar.activation(stat[:, 1, j:j + 1], stat[:, 0, j:j + 1], ACT.Ln, bias=eps[:, 0:1], scale=1.0 / D))
                nc.scalar.activation(stat[:, 2, j:j + 1], stat[:, 1, j:j + 1], ACT.Exp, scale=-0.5).then_inc(guessed, 1)

            def norm(to, at):
                for b in range(TB):
                    if to == "mem":
                        act.wait_ge(mem_in, 16)
                    elif at.x == 0:
                        act.wait_ge(tokens_in, 16)
                    else:
                        act.wait_ge(x_ready, at.x - 1 + b)
                    guess(mem_x[:, b, :] if to == "mem" else x[:, b, :], b, at)
                if to == "out":
                    return
                for b in range(TB):
                    for h in range(2):
                        act.wait_ge(xt_ready, at.turned + 2 * b + h + 1)
                        nc.scalar.activation((mem_h if to == "mem" else at_h)[:, 4 * h:4 * h + 4, b * P:(b + 1) * P],
                                             tiles(C[:, 2 * b + h, :], 4), ACT.Copy).then_inc(at_hi, 1)
                if to == "mem":
                    for n in range(AHEAD):
                        hi(n)

            def post(at):
                act.wait_ge(chunk_done, at.chunk)
                for b in range(TB):
                    guess(Y[:, 2 * b:2 * b + 2, :], b, at)

            def cols(specs, to, at):
                for i in range(len(specs)):
                    hi(at.chunk + i + AHEAD)
                    act.wait_ge(chunk_done, at.chunk + i + 1)
                    f = ACT.Silu if specs is even_cols and i >= 8 else ACT.Copy
                    nc.scalar.activation(to[i], tiles(C[:, i % 4, :], 2), f).then_inc(cols_copied, 1)

            def rows(at):
                for i in range(4):
                    hi(at.chunk + i + AHEAD)

            def relu_ff(at):
                n = at.chunk

                def units(j, t=None):
                    step = (lambda v: v) if t is None else (lambda v: t * 3 + v)
                    up = n if j == 0 else n + 2 * j - 1
                    act.wait_ge(chunk_done, up + 1 if t is None else t * 6 + (up + 1))
                    nc.scalar.activation(relu[j % 3], C[:, j % 3, :], ACT.Relu).then_inc(cols_copied, 1)
                    act.wait_ge(cols_copied, step(at.copied + j + 1))
                    nc.scalar.activation(full[j % 3], relu[j % 3], ACT.Square)
                    nc.scalar.activation(hid_h[:, j % 3, :], relu[j % 3], ACT.Square).then_inc(hid_hi, 1)

                hi(n + AHEAD)
                units(0)
                with nc.scalar.Fori(0, (N_REL - 1) // 3) as t:
                    for j in range(3):
                        hi(n + 1 + 2 * j + AHEAD, t)
                        units(j + 1, t)
                        hi(n + 2 + 2 * j + AHEAD, t)
                hi(n + 2 * N_REL - 1 + AHEAD)

            def swiglu(at):
                n = at.chunk

                def gate(j, t=None):
                    step = (lambda k, v: v) if t is None else (lambda k, v: t * k + v)
                    act.wait_ge(chunk_done, step(6, (n if j == 0 else n + 3 * j - 1) + 1))
                    nc.scalar.activation(relu[j % 2], C[:, 2 * (j % 2), :], ACT.Silu).then_inc(cols_copied, 1)

                hi(n + AHEAD)
                gate(0)
                hi(n + 1 + AHEAD)

                def three(j, t=None):
                    b = n + 2 + 3 * j + AHEAD
                    hi(b, t)
                    gate(j + 1, t)
                    hi(b + 1, t)
                    hi(b + 2, t)

                turns = glu_turns(n)
                with nc.scalar.Fori(0, turns) as t:
                    for j in range(2):
                        three(j, t)
                for j in range(2 * turns, N_GLU - 1):
                    three(j)
                hi(n + 3 * N_GLU - 1 + AHEAD)

            def contexts(i, at, kind):
                if kind == "stick":
                    act.wait_ge(weights_used, 2 * i + 2)
                else:
                    act.wait_ge(probs_used, at.head + (i + 1 if kind == "mem" else 2 * i + 2))
                if kind == "mem":
                    nc.scalar.activation(at_h[:, 2 * i:2 * i + 2, :], tiles(Y[:, i % 2, :], 2), ACT.Copy).then_inc(ctx_hi, 1)
                else:
                    nc.scalar.activation(at_h[:, i, :], Y[:, i % 2, 0:S], ACT.Copy).then_inc(ctx_hi, 1)

            def softmax(kind, heads, at):
                h0 = at.head
                for i in range(heads + 4):
                    if i < heads:
                        act.wait_ge(scores_max, h0 + i + 1)
                        if i >= 3:
                            act.wait_ge(probs_turned, h0 + i - 2)
                        for b, (first, end) in enumerate(rows_of(kind)):
                            j = 2 * i + b
                            src, size = (C[:, i % 2, :], 0.0625) if kind == "mem" else (sc[i % 2], 1.0)
                            last = nc.scalar.activation(pr[i % 3][:, first:end], src[:, first:end], ACT.Exp,
                                                        bias=a_stat[:, 0, j:j + 1], scale=size, accum_out=a_stat[:, 1, j:j + 1])
                        if kind == "swa":
                            last = nc.scalar.activation(a_stat[:, 3, 2 * i:2 * i + 2], a_stat[:, 0, 2 * i:2 * i + 2], ACT.Exp,
                                                        bias=sinks[:, i:i + 1])
                        last.then_inc(probs_ready, 1)
                    if 2 <= i < heads + 2:
                        k = i - 2
                        act.wait_ge(probs_turned, h0 + k + 1)
                        if k >= 2:
                            act.wait_ge(probs_used, h0 + k - 1)
                        width = rows_of(kind)[-1][1]
                        nc.scalar.activation(pT[k % 2][:, 0:width], C[:, 2 + k % 2, 0:width], ACT.Copy).then_inc(probs_copied, 1)
                    if i >= 3 and (kind == "mem" or i % 2 == 0) and i - 3 < heads:
                        contexts(i - 3 if kind == "mem" else (i - 3) // 2, at, kind)

            def rope(what, at):
                if what == "k":
                    act.wait_ge(kdup_ready, 1)
                    nc.scalar.activation(kdup, Y[:, 0:2, :].rearrange("p a (b c) -> p (a b) c", b=2), ACT.Copy).then_inc(kdup_copied, 1)

            def stick(at):
                for i in range(16 + 5):
                    if i < 16:
                        act.wait_ge(z_ready, i + 1)
                        if i >= 2:
                            act.wait_ge(keep_ready, i - 1)
                        soft = sc[i % 2][:, 0:SEEN]
                        again(nc.scalar.activation(soft, C[:, i % 2, 0:SEEN], ACT.Abs, scale=0.125))
                        again(nc.scalar.activation(soft, soft, ACT.Exp, scale=-1.0))
                        nc.scalar.activation(soft, soft, ACT.Ln, bias=1.0).then_inc(soft_ready, 1)
                    if 3 <= i < 16 + 3:
                        w = pT[(i - 3) % 3][:, 0:SEEN]
                        act.wait_ge(suffix_added, i - 2)
                        nc.scalar.activation(w, w, ACT.Exp).then_inc(weights_ready, 1)
                    if i >= 5 and i % 2 == 1:
                        contexts((i - 5) // 2, at, "stick")

            def even(at):
                f = f_t.rearrange(flat)
                act.wait_ge(lb_shifted, 1)
                nc.scalar.activation(not_lb, lb, ACT.Exp).then_inc(lb_exp, 1)
                act.wait_ge(clipped, 1)
                again(nc.scalar.activation(soft_f, f, ACT.Abs))
                again(nc.scalar.activation(soft_f, soft_f, ACT.Exp, scale=-1.0))
                nc.scalar.activation(exp_f, f, ACT.Exp, scale=-1.0)
                nc.scalar.activation(soft_f, soft_f, ACT.Ln, bias=1.0).then_inc(gates_exp, 1)
                act.wait_ge(lb_scaled, 1)
                nc.scalar.activation(xn[:, 0, :], xn[:, 0, :], ACT.Ln, bias=1.0).then_inc(gates_ln, 1)
                act.wait_ge(pool_ready, 1)
                nc.scalar.activation(pooled, C[:, 0:2, :].rearrange("p a (b c) -> p (a b) c", b=2), ACT.Copy).then_inc(pool_copied, 1)
                act.wait_ge(keys_turned, 1)
                for b in range(TB):
                    last = nc.scalar.activation(k_d[:, :, b * P:(b + 1) * P], tiles(Y[:, b, :], 4), ACT.Copy)
                last.then_inc(keys_copied, 1)
                act.wait_ge(mix_ready, 1)
                for g in range(4):
                    last = nc.scalar.activation(at_h[:, g, :], C[:, 2 + g // 2, g % 2 * S:(g % 2 + 1) * S], ACT.Copy,
                                                scale=pscale[:, g:g + 1])
                last.then_inc(mix_hi, 1)
                for l in range(1 + len(LEVELS)):
                    act.wait_ge(level_sum, l + 1)
                    if l >= 2:
                        act.wait_ge(level_both, l - 1)
                    bank = 2 * (l % 2)
                    nc.scalar.activation(tiles(fall[l % 2], 2), Y[:, bank:bank + 2, :], ACT.Exp).then_inc(level_exp, 1)
                act.wait_ge(rec_ready, 1)
                for b in range(TB):
                    last = nc.scalar.activation(xn[:, b, 512:1024], Y[:, b, :], ACT.Square)
                last.then_inc(rec_squared, 1)
                act.wait_ge(rec_meaned, 1)
                again(nc.scalar.activation(h_stat[:, 1, :], h_stat[:, 0, :], ACT.Ln, bias=eps[:, 0:1], scale=1.0 / P))
                nc.scalar.activation(h_stat[:, 2, :], h_stat[:, 1, :], ACT.Exp, scale=-0.5).then_inc(rec_guessed, 1)
                for b in range(TB):
                    act.wait_ge(rec_turned, b + 1)
                    nc.scalar.activation(at_h[:, 4:8, b * P:(b + 1) * P], tiles(C[:, b, :], 4), ACT.Copy).then_inc(rec_hi, 1)

            act.wait_ge(setup, 1)
            exp_and_ln()
            for s, at in before:
                if s[0] == "norm":
                    norm(s[1], at)
                elif s[0] == "post":
                    post(at)
                elif s[0] == "cols":
                    cols(s[1], s[2], at)
                    if s[1] is even_cols:
                        exp_and_ln()
                elif s[0] == "rows":
                    rows(at)
                elif s[0] == "relu_ff":
                    relu_ff(at)
                elif s[0] == "swiglu":
                    swiglu(at)
                    exp_and_ln()
                elif s[0] == "softmax":
                    softmax(s[1], s[2], at)
                elif s[0] == "rope":
                    rope(s[1], at)
                elif s[0] == "stick":
                    stick(at)
                elif s[0] == "even":
                    even(at)

        @block.vector
        def _(dve):
            V = nc.vector
            seq = [0]

            def again(ins):
                seq[0] += 1
                ins.then_inc(dve_seq, 1)
                dve.wait_ge(dve_seq, seq[0])

            def lo(n, t=None):
                if n >= N_CHUNKS:
                    return
                dve.wait_ge(hi_split, n + 1 if t is None else t * 6 + (n + 1))
                V.tensor_tensor(w_lo[:, n % RING, :], raw[:, n % RAW, :], w_hi[:, n % RING, :].bitcast(f32),
                                ALU.subtract).then_inc(lo_split, 1)

            def newton(guess, squares, scratch, size):
                again(V.tensor_scalar(scratch[0], squares, size, EPS, ALU.mult, ALU.add))
                again(V.tensor_tensor(scratch[1], guess, guess, ALU.mult))
                again(V.tensor_tensor(scratch[1], scratch[1], scratch[0], ALU.mult))
                again(V.tensor_scalar(scratch[2], scratch[1], -0.5, 1.5, ALU.mult, ALU.add))
                again(V.tensor_tensor(scratch[3], guess, scratch[2], ALU.mult))

            def rms(b, at):
                j = 2 * at.norm + b
                dve.wait_ge(guessed, j + 1)
                newton(stat[:, 2, j:j + 1], stat[:, 0, j:j + 1], [stat[:, k, j:j + 1] for k in range(3, 7)], 1.0 / D)
                return stat[:, 6, j:j + 1]

            def scaled(src, b, at):
                r = rms(b, at)
                dve.wait_ge(gains_in[at.norm % 2], 16 * (at.norm // 2 + 1))
                return V.scalar_tensor_tensor(xn[:, b, :], src, r, gain[:, at.norm % 2, :], ALU.mult, ALU.mult)

            def norm(to, at):
                for b in range(TB):
                    last = scaled(mem_x[:, b, :] if to == "mem" else x[:, b, :], b, at)
                    last.then_inc(xn_ready, 1)
                if to == "out":
                    return
                h, l = (mem_h, mem_l) if to == "mem" else (at_h, at_l)
                for b in range(TB):
                    for k in range(2):
                        dve.wait_ge(at_hi, at.turned + 2 * b + k + 1)
                        part = (slice(None), slice(4 * k, 4 * k + 4), slice(b * P, (b + 1) * P))
                        V.tensor_tensor(l[part], tiles(C[:, 2 * b + k, :], 4), h[part].bitcast(f32),
                                        ALU.subtract).then_inc(at_lo, 1)
                if to == "mem":
                    for n in range(AHEAD):
                        lo(n)

            def post(at):
                for b in range(TB):
                    again(scaled(Y[:, 2 * b:2 * b + 2, :].rearrange(flat), b, at))
                    last = V.tensor_tensor(x[:, b, :], x[:, b, :], xn[:, b, :], ALU.add)
                    last.then_inc(x_ready, 1)

            def add(factor, at):
                dve.wait_ge(chunk_done, at.chunk)
                for b in range(TB):
                    V.scalar_tensor_tensor(x[:, b, :], Y[:, 2 * b:2 * b + 2, :].rearrange(flat), factor, x[:, b, :],
                                           ALU.mult, ALU.add).then_inc(x_ready, 1)

            def cols(n, at):
                for i in range(n):
                    lo(at.chunk + i + AHEAD)

            def relu_ff(at):
                n = at.chunk

                def units(j, t=None):
                    dve.wait_ge(hid_hi, at.hid_hi + j + 1 if t is None else t * 3 + (at.hid_hi + j + 1))
                    V.tensor_tensor(hid_l[:, j % 3, :], full[j % 3], hid_h[:, j % 3, :].bitcast(f32),
                                    ALU.subtract).then_inc(hid_lo, 1)

                lo(n + AHEAD)
                units(0)
                with nc.vector.Fori(0, (N_REL - 1) // 3) as t:
                    for j in range(3):
                        lo(n + 1 + 2 * j + AHEAD, t)
                        units(j + 1, t)
                        lo(n + 2 + 2 * j + AHEAD, t)
                lo(n + 2 * N_REL - 1 + AHEAD)

            def swiglu(at):
                n = at.chunk

                def units(j, t=None):
                    step = (lambda k, v: v) if t is None else (lambda k, v: t * k + v)
                    dve.wait_ge(chunk_done, step(6, (n if j == 0 else n + 3 * j - 1) + 2))
                    dve.wait_ge(cols_copied, step(2, at.copied + j + 1))
                    up = C[:, 2 * (j % 2) + 1, :]
                    V.tensor_tensor(full[j % 2], up, relu[j % 2], ALU.mult)
                    V.tensor_tensor(hid_h[:, j % 2, :], up, relu[j % 2], ALU.mult).then_inc(up_used, 1)
                    dve.wait_ge(up_used, step(2, at.up + j + 1))
                    V.tensor_tensor(hid_l[:, j % 2, :], full[j % 2], hid_h[:, j % 2, :].bitcast(f32),
                                    ALU.subtract).then_inc(hid_lo, 1)

                lo(n + AHEAD)
                lo(n + 1 + AHEAD)
                units(0)

                def three(j, t=None):
                    b = n + 2 + 3 * j + AHEAD
                    lo(b, t)
                    lo(b + 1, t)
                    units(j + 1, t)
                    lo(b + 2, t)

                turns = glu_turns(n)
                with nc.vector.Fori(0, turns) as t:
                    for j in range(2):
                        three(j, t)
                for j in range(2 * turns, N_GLU - 1):
                    three(j)
                lo(n + 3 * N_GLU - 1 + AHEAD)

            def contexts(i, at, kind):
                dve.wait_ge(ctx_hi, at.ctx + i + 1)
                if kind == "mem":
                    V.tensor_tensor(at_l[:, 2 * i:2 * i + 2, :], tiles(Y[:, i % 2, :], 2),
                                    at_h[:, 2 * i:2 * i + 2, :].bitcast(f32), ALU.subtract).then_inc(ctx_lo, 1)
                else:
                    V.tensor_tensor(at_l[:, i, :], Y[:, i % 2, 0:S], at_h[:, i, :].bitcast(f32),
                                    ALU.subtract).then_inc(ctx_lo, 1)

            def softmax(kind, heads, at):
                h0 = at.head
                rows = rows_of(kind)
                for i in range(heads + 5):
                    if i < heads:
                        two = slice(2 * i, 2 * i + 2)
                        dve.wait_ge(scores_ready, h0 + i + 1)
                        if i >= 2:
                            dve.wait_ge(probs_ready, h0 + i - 1)
                        if kind == "mem":
                            ins = V.reduce_max(a_stat[:, 4, two], tiles(C[:, i % 2, :], 2), X)
                        else:
                            for b, (first, end) in enumerate(rows):
                                ins = V.tensor_tensor_reduce(
                                    out=sc[i % 2][:, first:end], in0=C[:, i % 2, first:end], in1=mask[:, first:end], scale=0.125,
                                    scalar=LOWEST, op0=ALU.add, op1=ALU.max, accum_out=a_stat[:, 4, 2 * i + b:2 * i + b + 1])
                        ins.then_inc(scores_scaled, 1)
                        dve.wait_ge(scores_scaled, h0 + i + 1)
                        if kind == "swa":
                            V.tensor_scalar(a_stat[:, 0, two], a_stat[:, 4, two], -1.0, sinks[:, 16 + i:17 + i], ALU.mult,
                                            ALU.min).then_inc(scores_max, 1)
                        else:
                            V.tensor_scalar(a_stat[:, 0, two], a_stat[:, 4, two], -0.0625 if kind == "mem" else -1.0, None,
                                            ALU.mult).then_inc(scores_max, 1)
                    if 1 <= i <= heads:
                        k = i - 1
                        two = slice(2 * k, 2 * k + 2)
                        dve.wait_ge(probs_ready, h0 + k + 1)
                        if kind == "swa":
                            again(V.tensor_tensor(a_stat[:, 1, two], a_stat[:, 1, two], a_stat[:, 3, two], ALU.add))
                        again(V.reciprocal(a_stat[:, 2, two], a_stat[:, 1, two]))
                        for b, (first, end) in enumerate(rows):
                            p = pr[k % 3][:, first:end]
                            last = V.tensor_scalar(p, p, a_stat[:, 2, 2 * k + b:2 * k + b + 1], None, ALU.mult)
                        last.then_inc(probs_scaled, 1)
                    if i >= 4 and (kind == "mem" or i % 2 == 1) and i - 4 < heads:
                        contexts(i - 4 if kind == "mem" else (i - 4) // 2, at, kind)

            def rope_(what, n, at):
                t = qT if what == "q" else kT
                cos, sin = (rope[:, i:i + 1, :].broadcast_to([P, 2, S]) for i in range(2))
                if what == "k":
                    dve.wait_ge(swa_in, 16 * 7)
                    V.tensor_scalar(sinks[:, 16:32], sinks[:, 0:16], -1.0, None, ALU.mult).then_inc(sink_ready, 1)
                    dve.wait_ge(sink_ready, 1)
                for c in range(n):
                    dve.wait_ge(turned, at.rot + c + 1)
                    if c >= 1:
                        dve.wait_ge(rotated, at.rot + c)
                    V.tensor_tensor(tiles(rot[0], 2), halves(t, c), cos, ALU.mult)
                    again(V.tensor_tensor(tiles(rot[1], 2), tiles(Y[:, c, :], 2), sin, ALU.mult))
                    V.tensor_tensor(halves(t, c), tiles(rot[0], 2), tiles(rot[1], 2), ALU.add).then_inc(rotated, 1)

            def stick(at):
                for i in range(16 + 6):
                    if 1 <= i <= 16:
                        h = i - 1
                        k = h % 2
                        beta, z = bias[k][:, 0:SEEN], C[:, k, 0:SEEN]
                        dve.wait_ge(soft_ready, h + 1)
                        if h >= 2:
                            dve.wait_ge(suffix_ready, h - 1)
                            dve.wait_ge(suffix_added, h - 1)
                        again(V.tensor_scalar(beta, z, 0.125, 0.0, ALU.mult, ALU.min))
                        again(V.tensor_tensor(beta, beta, sc[k][:, 0:SEEN], ALU.subtract))
                        V.scalar_tensor_tensor(pr[k][:, 0:SEEN], z, -0.125, beta, ALU.mult, ALU.add).then_inc(keep_ready, 1)
                    if 2 <= i < 16 + 2:
                        h = i - 2
                        dve.wait_ge(suffix_ready, h + 1)
                        if h >= 3:
                            dve.wait_ge(weights_used, h - 2)
                        V.tensor_tensor(pT[h % 3][:, 0:SEEN], C[:, 2 + h % 2, 0:SEEN], bias[h % 2][:, 0:SEEN],
                                        ALU.add).then_inc(suffix_added, 1)
                    if i >= 6 and i % 2 == 0:
                        contexts((i - 6) // 2, at, "stick")

            def even(at):
                f = f_t.rearrange(flat)
                dve.wait_ge(even_in, 16 * 8)
                V.tensor_tensor(lb, lb, lb, ALU.subtract).then_inc(lb_shifted, 1)
                dve.wait_ge(cols_copied, at.copied)
                V.tensor_scalar(f, f, GATE_CLIP, -GATE_CLIP, ALU.min, ALU.max).then_inc(clipped, 1)
                dve.wait_ge(lb_exp, 1)
                again(V.reciprocal(lb, not_lb))
                again(V.tensor_tensor(not_lb, not_lb, lb, ALU.mult))
                again(V.tensor_tensor(lb, not_lb, not_lb, ALU.subtract))
                again(V.tensor_scalar(lb, lb, 0.0, 1.0, ALU.max, ALU.min))
                V.tensor_scalar(not_lb, lb, -1.0, 1.0, ALU.mult, ALU.add)
                again(V.tensor_tensor(g_t.rearrange("p b (h d) -> p (b h) d", h=4), g_t.rearrange("p b (h d) -> p (b h) d", h=4),
                                      og[:, None, :].broadcast_to([P, 8, P]), ALU.mult))
                dve.wait_ge(gates_exp, 1)
                by_block = lambda t: t[:, None, :].broadcast_to([P, TB, 512])
                V.tensor_tensor(tiles(xn[:, 0, :], 2), tiles(exp_f, 2), by_block(lb), ALU.mult).then_inc(lb_scaled, 1)
                again(V.tensor_scalar(key, exp_f, 1.0, None, ALU.add))
                again(V.reciprocal(key, key))
                again(V.tensor_tensor(key, key, exp_f, ALU.mult))
                V.tensor_tensor(tiles(key, 2), tiles(key, 2), by_block(not_lb), ALU.mult).then_inc(keys_ready, 1)
                again(V.scalar_tensor_tensor(f, f, 0.0, soft_f, ALU.min, ALU.subtract))
                dve.wait_ge(gates_ln, 1)
                V.tensor_tensor(f, f, xn[:, 0, :], ALU.add).then_inc(decays_ready, 1)
                dve.wait_ge(mix_hi, 1)
                for g in range(4):
                    last = V.scalar_tensor_tensor(at_l[:, g, :], C[:, 2 + g // 2, g % 2 * S:(g % 2 + 1) * S], pscale[:, g:g + 1],
                                                  at_h[:, g, :].bitcast(f32), ALU.mult, ALU.subtract)
                last.then_inc(mix_lo, 1)
                dve.wait_ge(level_score, 1)
                for b in range(TB):
                    last = V.tensor_tensor(score[b], tiles(C[:, b, :], 4), ident[:, None, :].broadcast_to([P, 4, P]), ALU.mult)
                last.then_inc(level_used, 1)
                for l in range(2 + len(LEVELS)):
                    if l < 1 + len(LEVELS):
                        dve.wait_ge(level_exp, l + 1)
                        if l >= 2:
                            dve.wait_ge(level_score, l)
                        m = P if l == 0 else LEVELS[l - 1]
                        by_half = lambda t, k: t.rearrange(flat).rearrange("p (j two m) -> p j two m", two=2, m=m)[:, :, k, :]
                        decay = tiles(fall[l % 2], 4)
                        V.tensor_tensor(by_half(both[l % 2], 0), by_half(k_d, 0), by_half(decay, 0), ALU.mult)
                        V.tensor_tensor(by_half(both[l % 2], 1), by_half(q_d, 1), by_half(decay, 1), ALU.mult).then_inc(level_both, 1)
                    if l >= 1:
                        dve.wait_ge(level_score, l + 1)
                        bank = 2 * (l % 2)
                        if l == 1:
                            V.tensor_copy(score[2], tiles(C[:, bank, :], 4)).then_inc(level_used, 1)
                        else:
                            pairs = pair_c[:, (l - 2) * P:(l - 1) * P].bitcast(i32)[:, None, :].broadcast_to([P, 4, P])
                            dve.wait_ge(level_used, l)
                            for b in range(TB):
                                last = V.copy_predicated(score[b], pairs, tiles(C[:, bank + b, :], 4))
                            last.then_inc(level_used, 1)
                dve.wait_ge(rec_squared, 1)
                for b in range(TB):
                    last = V.reduce_sum(h_stat[:, 0, 4 * b:4 * b + 4], tiles(xn[:, b, 512:1024], 4), X)
                last.then_inc(rec_meaned, 1)
                dve.wait_ge(rec_guessed, 1)
                newton(h_stat[:, 2, :], h_stat[:, 0, :], [h_stat[:, k, :] for k in range(3, 7)], 1.0 / P)
                for b in range(TB):
                    r = h_stat[:, 6, 4 * b:4 * b + 4][:, :, None].broadcast_to([P, 4, P])
                    again(V.tensor_tensor(tiles(xn[:, b, 0:512], 4), tiles(Y[:, b, :], 4), r, ALU.mult))
                    V.tensor_tensor(xn[:, b, 0:512], xn[:, b, 0:512], g_t[:, b, :], ALU.mult).then_inc(rec_normed, 1)
                for b in range(TB):
                    dve.wait_ge(rec_hi, b + 1)
                    part = (slice(None), slice(4, 8), slice(b * P, (b + 1) * P))
                    V.tensor_tensor(at_l[part], tiles(C[:, b, :], 4), at_h[part].bitcast(f32), ALU.subtract).then_inc(rec_lo, 1)

            dve.wait_ge(ident_in, 16)
            for s, at in before:
                if s[0] == "norm":
                    norm(s[1], at)
                elif s[0] == "post":
                    post(at)
                elif s[0] == "add":
                    add(s[1], at)
                elif s[0] == "cols":
                    cols(len(s[1]), at)
                elif s[0] == "rows":
                    cols(4, at)
                elif s[0] == "relu_ff":
                    relu_ff(at)
                elif s[0] == "swiglu":
                    swiglu(at)
                elif s[0] == "softmax":
                    softmax(s[1], s[2], at)
                elif s[0] == "rope":
                    rope_(s[1], s[2], at)
                elif s[0] == "stick":
                    stick(at)
                elif s[0] == "even":
                    even(at)

        @block.tensor
        def _(pe):
            mm = nc.tensor.matmul

            def split_ready(n, t=None):
                pe.wait_ge(lo_split, n + 1 if t is None else t * 6 + (n + 1))

            def col_chunk(n, kind, h, l, bank, t=None):
                split_ready(n, t)
                wh, wl = (w[:, n % RING, :].rearrange("p (k c) -> p k c", k=KT) for w in (w_hi, w_lo))
                for i in range(2):
                    part = slice(i * P, (i + 1) * P)
                    to = C[:, bank, i * S:(i + 1) * S]
                    for k in range(KT):
                        if kind == "T":
                            passes = ((wh[:, k, part], h[:, k, :]), (wh[:, k, part], l[:, k, :]), (wl[:, k, part], h[:, k, :]))
                        else:
                            passes = ((h[:, k, part], wh[:, k, :]), (h[:, k, part], wl[:, k, :]), (l[:, k, part], wh[:, k, :]))
                        for j, (still, moving) in enumerate(passes):
                            last = mm(to, still, moving, start=k == 0 and j == 0, stop=k == KT - 1 and j == 2)
                last.then_inc(chunk_done, 1)

            def row_chunk(n, h, l, first, end, t=None):
                split_ready(n, t)
                wh, wl = (w[:, n % RING, :].rearrange("p (k c) -> p k c", k=2) for w in (w_hi, w_lo))
                for k in range(2):
                    for b in range(TB):
                        part = slice(b * P, (b + 1) * P)
                        for still, moving, j in ((h[k], wh, 0), (h[k], wl, 1), (l[k], wh, 2)):
                            for half in range(2):
                                last = mm(Y[:, 2 * b + half, :], still[:, part], moving[:, k, half * 512:(half + 1) * 512],
                                          start=first and k == 0 and j == 0, stop=end and k == 1 and j == 2)
                last.then_inc(chunk_done, 1)

            def cols(specs, at):
                pe.wait_ge(at_lo, at.turned)
                for i, (_, _, _, kind, src) in enumerate(specs):
                    if i >= 4:
                        pe.wait_ge(cols_copied, at.copied + i - 3)
                    h, l = (mem_h, mem_l) if src == "mem" else (at_h, at_l)
                    col_chunk(at.chunk + i, kind, h, l, i % 4)

            def rows(at):
                for r in range(4):
                    row_chunk(at.chunk + r, [at_h[:, 2 * r + k, :] for k in range(2)], [at_l[:, 2 * r + k, :] for k in range(2)],
                                     r == 0, r == 3)

            def norm(at):
                for b in range(TB):
                    pe.wait_ge(xn_ready, at.xn + b + 1)
                    for h in range(2):
                        for k in range(4):
                            last = nc.tensor.transpose(C[:, 2 * b + h, k * P:(k + 1) * P],
                                                       xn[:, b, (4 * h + k) * P:(4 * h + k + 1) * P], ident[:])
                        last.then_inc(xt_ready, 1)

            def clear_y():
                for i in range(4):
                    mm(Y[:, i, :], zeros[:, 0:P], zeros[:], start=True, stop=False)

            def hidden(slot):
                return [[t[:, slot, k * S:(k + 1) * S] for k in range(2)] for t in (hid_h, hid_l)]

            def relu_ff(at):
                n = at.chunk
                pe.wait_ge(at_lo, at.turned)

                def up(j, t=None):
                    col_chunk(n if j == 0 else n + 2 * j - 1, "T", at_h, at_l, j % 3, t)

                def down(j, t=None, end=False):
                    pe.wait_ge(hid_lo, at.hid + j + 1 if t is None else t * 3 + (at.hid + j + 1))
                    row_chunk(n + 2 * N_REL - 1 if end else n + 2 * j + 2, *hidden(j % 3), False, end, t)

                clear_y()
                up(0)
                with nc.tensor.Fori(0, (N_REL - 1) // 3) as t:
                    for j in range(3):
                        up(j + 1, t)
                        down(j, t)
                down(N_REL - 1, end=True)

            def swiglu(at):
                n = at.chunk
                pe.wait_ge(at_lo, at.turned)

                def gate_up(j, t=None):
                    first = n if j == 0 else n + 3 * j - 1
                    col_chunk(first, "T", at_h, at_l, 2 * (j % 2), t)
                    col_chunk(first + 1, "T", at_h, at_l, 2 * (j % 2) + 1, t)

                def down(j, t=None, end=False):
                    pe.wait_ge(hid_lo, at.hid + j + 1 if t is None else t * 2 + (at.hid + j + 1))
                    row_chunk(n + 3 * N_GLU - 1 if end else n + 3 * j + 4, *hidden(j % 2), False, end, t)

                clear_y()
                gate_up(0)
                with nc.tensor.Fori(0, (N_GLU - 1) // 2) as t:
                    for j in range(2):
                        gate_up(j + 1, t)
                        down(j, t)
                down(N_GLU - 1, end=True)

            def half_of(t, h):
                return t[64 * (h % 2):64 * (h % 2) + 64, h // 2, :]

            def context(i, values, weights, used):
                rows, bank = slice(64 * (i % 2), 64 * (i % 2) + 64), (i // 2) % 2
                mm(Y[rows, bank, 0:S], values(0), weights[:, 0:S], start=True, stop=False)
                mm(Y[rows, bank, P:S], values(1), weights[:, S:SEEN], start=False, stop=True).then_inc(used, 1)

            def softmax(kind, heads, at):
                h0 = at.head
                pe.wait_ge(cols_copied, at.copied)
                if kind == "swa":
                    pe.wait_ge(rotated, at.rot)
                if kind == "band":
                    pe.wait_ge(band_in, 32)
                for i in range(heads + 3):
                    if i < heads:
                        if i >= 2:
                            pe.wait_ge(probs_ready if kind == "mem" else scores_scaled, h0 + i - 1)
                        if kind == "band":
                            pe.wait_ge(bias_in[i % 2], 32 * (i // 2 + 1))
                        for b, (first, end) in enumerate(rows_of(kind)):
                            q, keys = slice(b * P, (b + 1) * P), slice(0, end - first)
                            to = C[:, i % 2, first:end]
                            if kind == "mem":
                                for k in range(2):
                                    last = mm(to, qT[:, 2 * i + k, q], kT[:, 2 * i + k, :], start=k == 0, stop=k == 1)
                            elif kind == "band":
                                mm(to, half_of(qT, i)[:, q], half_of(kT, i)[:, keys], start=True, stop=False)
                                last = mm(to, flip_c, bias[i % 2][:, first:end], start=False, stop=True)
                            else:
                                part = slice(64 * (i % 2), 64 * (i % 2) + 64)
                                last = mm(to, half_of(qT, i)[:, q], kdup[part, i // 4, keys], start=True, stop=True)
                        last.then_inc(scores_ready, 1)
                    if 2 <= i < heads + 2:
                        k = i - 2
                        pe.wait_ge(probs_scaled, h0 + k + 1)
                        if k >= 2:
                            pe.wait_ge(probs_copied, h0 + k - 1)
                        turn = ((0, 0), (1, 2), (2, 1), (3, 3)) if kind == "mem" else ((0, 0), (1, 1), (2, 2))
                        for to, src in turn:
                            last = nc.tensor.transpose(C[:, 2 + k % 2, to * P:(to + 1) * P], pr[k % 3][:, src * P:(src + 1) * P], ident[:])
                        last.then_inc(probs_turned, 1)
                    if i >= 3:
                        k = i - 3
                        pe.wait_ge(probs_copied, h0 + k + 1)
                        if kind == "mem":
                            if k >= 2:
                                pe.wait_ge(ctx_lo, at.ctx + k - 1)
                            for half in range(2):
                                for kb in range(2):
                                    first = k * S + half * P
                                    last = mm(Y[:, k % 2, half * S:(half + 1) * S], vt[:, kb, first:first + P],
                                              pT[k % 2][:, kb * S:(kb + 1) * S], start=kb == 0, stop=kb == 1)
                            last.then_inc(probs_used, 1)
                        else:
                            if k >= 4 and k % 2 == 0:
                                pe.wait_ge(ctx_lo, at.ctx + k // 2 - 1)
                            head = k if kind == "band" else k // 4
                            context(k, lambda kb: vt[:, kb, head * 64:head * 64 + 64], pT[k % 2], probs_used)
                pe.wait_ge(ctx_lo, at.ctx + (4 if kind == "mem" else 8))

            def rope_(what, n, at):
                t = qT if what == "q" else kT
                pe.wait_ge(cols_copied, at.copied)
                pe.wait_ge(swa_in, 16 * 7)
                for c in range(n):
                    mm(Y[:, c, :], turn_c, halves(t, c), start=True, stop=True).then_inc(turned, 1)
                if what == "k":
                    pe.wait_ge(rotated, at.rot + 1)
                    for h in range(4):
                        last = mm(Y[:, h // 2, h % 2 * S:(h % 2 + 1) * S], low_c if h % 2 == 0 else high_c, kT[:, h // 2, :],
                                  start=True, stop=True)
                    last.then_inc(kdup_ready, 1)
                    pe.wait_ge(kdup_copied, 1)

            def stick(at):
                pe.wait_ge(cols_copied, at.copied)
                pe.wait_ge(stick_in, 48)
                for i in range(16 + 4):
                    if i < 16:
                        if i >= 2:
                            pe.wait_ge(keep_ready, i - 1)
                        mm(C[:, i % 2, 0:S], half_of(kT, i)[:, 0:P], half_of(qT, i), start=True, stop=True)
                        mm(C[:, i % 2, S:SEEN], half_of(kT, i)[:, P:S], half_of(qT, i)[:, P:S], start=True,
                           stop=True).then_inc(z_ready, 1)
                    if 2 <= i < 16 + 2:
                        h = i - 2
                        keep, bank = pr[h % 2], 2 + h % 2
                        pe.wait_ge(keep_masked, h + 1)
                        if h >= 2:
                            pe.wait_ge(suffix_added, h - 1)
                        mm(C[:, bank, 0:S], after_s, keep[:, 0:S], start=True, stop=False)
                        mm(C[:, bank, P:S], ones_s, keep[:, S:SEEN], start=False, stop=True)
                        mm(C[:, bank, S:SEEN], after_s, keep[:, S:SEEN], start=True, stop=True).then_inc(suffix_ready, 1)
                    if i >= 4:
                        h = i - 4
                        pe.wait_ge(weights_masked, h + 1)
                        if h >= 4 and h % 2 == 0:
                            pe.wait_ge(ctx_lo, at.ctx + h // 2 - 1)
                        context(h, lambda kb: vt[:, kb, h * 64:h * 64 + 64], pT[h % 3], weights_used)
                pe.wait_ge(ctx_lo, at.ctx + 8)

            def even(at):
                pe.wait_ge(cols_copied, at.copied)
                pe.wait_ge(pool_in, 32)
                pe.wait_ge(even_in, 16 * 8)
                for g in range(4):
                    for b in range(TB):
                        table = pool_c[g // 2][:, (g % 2 * 2 + b) * S:(g % 2 * 2 + b + 1) * S]
                        last = mm(C[:, g // 2, g % 2 * S:(g % 2 + 1) * S], u_t[:, b, g * P:(g + 1) * P], table,
                                  start=b == 0, stop=b == 1)
                last.then_inc(pool_ready, 1)
                pe.wait_ge(keys_ready, 1)
                for b in range(TB):
                    for h in range(4):
                        last = nc.tensor.transpose(Y[:, b, h * P:(h + 1) * P], tiles(key, 8)[:, 4 * b + h, :], ident[:])
                last.then_inc(keys_turned, 1)
                pe.wait_ge(pool_copied, 1)
                for g in range(4):
                    last = mm(C[:, 2 + g // 2, g % 2 * S:(g % 2 + 1) * S], pool_w[:, g, :], pooled[:, g, :], start=True, stop=True)
                last.then_inc(mix_ready, 1)
                pe.wait_ge(keys_copied, 1)
                for b in range(TB):
                    part = slice(b * P, (b + 1) * P)
                    for h in range(4):
                        last = mm(C[:, b, h * P:(h + 1) * P], k_d[:, h, part], q_d[:, h, part], start=True, stop=True)
                last.then_inc(level_score, 1)
                pe.wait_ge(decays_ready, 1)
                pe.wait_ge(mix_lo, 1)
                for l in range(2 + len(LEVELS)):
                    if l < 1 + len(LEVELS):
                        if l >= 2:
                            pe.wait_ge(level_exp, l - 1)
                        for h in range(4):
                            for b in range(TB):
                                table = (after_c, upto_c)[b] if l == 0 else span_c[:, (l - 1) * P:l * P]
                                to = h % 2 * S + b * P
                                last = mm(Y[:, 2 * (l % 2) + h // 2, to:to + P], f_t[:, b, h * P:(h + 1) * P], table,
                                          start=True, stop=True)
                        last.then_inc(level_sum, 1)
                    if l >= 1:
                        pe.wait_ge(level_both, l)
                        pe.wait_ge(level_used, l - 1 if l >= 2 else 1)
                        qk = both[(l - 1) % 2]
                        bank = 2 * (l % 2)
                        for b in range(1 if l == 1 else TB):
                            for h in range(4):
                                keys = qk[:, h, 0:P] if l == 1 else qk[:, h, b * P:(b + 1) * P]
                                queries = qk[:, h, P:S] if l == 1 else keys
                                last = mm(C[:, bank + b, h * P:(h + 1) * P], keys, queries, start=True, stop=True)
                        last.then_inc(level_score, 1)
                pe.wait_ge(level_used, 2 + len(LEVELS))
                pe.wait_ge(level_exp, 1 + len(LEVELS))
                for b in range(TB):
                    for h in range(4):
                        head = slice(h * P, (h + 1) * P)
                        if b == 1:
                            mm(Y[:, b, head], score[2][:, h, :], v_t[:, 0, head], start=True, stop=False)
                        last = mm(Y[:, b, head], score[b][:, h, :], v_t[:, b, head], start=b == 0, stop=True)
                last.then_inc(rec_ready, 1)
                for b in range(TB):
                    pe.wait_ge(rec_normed, b + 1)
                    for h in range(4):
                        last = nc.tensor.transpose(C[:, b, h * P:(h + 1) * P], xn[:, b, h * P:(h + 1) * P], ident[:])
                    last.then_inc(rec_turned, 1)
                pe.wait_ge(rec_lo, TB)

            pe.wait_ge(ident_in, 16)
            pe.wait_ge(setup, 1)
            for s, at in before:
                if s[0] == "norm" and s[1] != "out":
                    norm(at)
                elif s[0] == "cols":
                    cols(s[1], at)
                elif s[0] == "rows":
                    rows(at)
                elif s[0] == "relu_ff":
                    relu_ff(at)
                elif s[0] == "swiglu":
                    swiglu(at)
                elif s[0] == "softmax":
                    softmax(s[1], s[2], at)
                elif s[0] == "rope":
                    rope_(s[1], s[2], at)
                elif s[0] == "stick":
                    stick(at)
                elif s[0] == "even":
                    even(at)


def kernel(**inputs):
    import concourse.bacc as bacc
    from concourse.bass_utils import run_bass_kernel_spmd

    nc = bacc.Bacc("TRN2", target_bir_lowering=False, num_devices=1)
    arrays, args = {}, {}
    data = {k: np.ascontiguousarray(v) for k, v in inputs.items() if k not in ("rel_bias", "pool_scale")}
    data["pool_scale_by_group"] = np.ascontiguousarray(np.asarray(inputs["pool_scale"]).reshape(4, P).T)
    data["rel_reversed"] = np.ascontiguousarray(np.asarray(inputs["rel_bias"])[0, :, ::-1])
    data.update(constants())
    for name, v in data.items():
        arrays["in_" + name] = v
        args[name] = nc.dram_tensor("in_" + name, v.shape, mybir.dt.from_np(v.dtype), kind="ExternalInput").ap()
    out = nc.dram_tensor("out_0", (1, S, D), mybir.dt.float32, kind="ExternalOutput").ap()
    build(nc, args, out)
    r = run_bass_kernel_spmd(nc, [arrays], core_ids=[0])
    return r.results[0]["out_0"]
```

```python
from contextlib import ExitStack

import numpy as np

import concourse.bass as bass
from concourse import mybir

P = 128
S = 256
TB = S // P
D = 1024
KT = D // P
CH = 256
RAW = 3
RING = 3
AHEAD = RING - 1
EPS = 1e-6
NEG = -1e30
LOWEST = -3e38
REL = 256
FF = 4096
DFF = 2816
LEVELS = (64, 32, 16, 8, 4, 2, 1)
POOL_WINDOWS = (2, 4, 8, 16)
GATE_CLIP = 60.0
N_NORMS = 24
WARM_START, WARM_POST, WARM_ADD, WARM_BLOCK = 20, 26, 10, 3


class Counts:

    def __init__(self, norm, rms, xn, turned, x, y, chunk, copied, hid, hid_hi, up, head, ctx, rot):
        self.norm, self.rms, self.xn, self.turned, self.x, self.y = norm, rms, xn, turned, x, y
        self.chunk, self.copied = chunk, copied
        self.hid, self.hid_hi, self.up, self.head, self.ctx, self.rot = hid, hid_hi, up, head, ctx, rot


def constants():
    i = np.arange(P)
    t = {}
    t["ident"] = np.eye(P)
    t["after"] = (i[:, None] > i[None, :])
    t["upto"] = (i[:, None] <= i[None, :])
    span, pair = [], []
    for m in LEVELS:
        half = (i // m) % 2
        mid = (i // (2 * m)) * 2 * m + m - 1
        tau, tok = i[:, None], i[None, :]
        right = (half[None, :] == 1) & (tau > mid[None, :]) & (tau <= tok)
        left = (half[None, :] == 0) & (tau > tok) & (tau <= mid[None, :])
        span.append(right | left)
        same = (i[:, None] // (2 * m)) == (i[None, :] // (2 * m))
        pair.append(same & (half[:, None] == 0) & (half[None, :] == 1))
    t["span"] = np.concatenate(span, 1)
    t["pair"] = np.concatenate(pair, 1)
    tok = np.arange(S)
    pool = []
    for w in POOL_WINDOWS:
        for b in range(TB):
            tau = b * P + i[:, None]
            inside = (tau <= tok[None, :]) & (tau > tok[None, :] - w)
            count = np.minimum(tok + 1, w).astype(np.float32)[None, :]
            pool.append(inside / count - (tau == tok[None, :]))
    t["pool"] = np.concatenate(pool, 1)
    q = tok.reshape(TB, P)
    band, swa = [], []
    for b in range(TB):
        qq = q[b][:, None]
        kk = tok[None, :]
        seen = slice(0, (b + 1) * P)
        band.append(np.where(kk // 64 <= qq // 64, 0.0, NEG)[:, seen])
        swa.append(np.where((qq - kk >= 0) & (qq - kk < 128), 0.0, NEG)[:, seen])
    t["band"] = np.concatenate(band, 1)
    t["swa"] = np.concatenate(swa, 1)
    t["strict"] = (i[:, None] < i[None, :])
    half = 32
    freq = np.float32(10000.0) ** (-np.arange(half, dtype=np.float32) / np.float32(half))
    ang = tok.astype(np.float32)[None, :] * freq[:, None].astype(np.float32)
    t["cos"] = np.tile(np.cos(ang), (4, 1))
    t["sin"] = np.tile(np.sin(ang), (4, 1))
    turn = np.zeros((P, P))
    for d in range(P):
        if d % 64 < half:
            turn[d + half, d] = -1.0
        else:
            turn[d - half, d] = 1.0
    t["turn"] = turn
    t["low"] = np.concatenate([np.eye(64), np.zeros((64, 64))], 0) @ np.concatenate([np.eye(64), np.eye(64)], 1)
    t["high"] = np.concatenate([np.zeros((64, 64)), np.eye(64)], 0) @ np.concatenate([np.eye(64), np.eye(64)], 1)
    t["flip"] = 8.0 * np.eye(P)[::-1]
    t["ones"] = np.ones((P, P))
    return {k: np.ascontiguousarray(v, dtype=np.float32) for k, v in t.items()}


def build(nc, a, out):
    f32 = mybir.dt.float32
    f32r = mybir.dt.float32r
    bf16 = mybir.dt.bfloat16
    i32 = mybir.dt.int32
    ACT = mybir.ActivationFunctionType
    ALU = mybir.AluOpType
    X = mybir.AxisListType.X
    ctx = ExitStack()

    def sb(name, shape, dt=f32):
        return ctx.enter_context(nc.sbuf_tensor(name, shape, dt))

    def sem(name):
        return ctx.enter_context(nc.semaphore(name))

    with ctx:
        raw = sb("raw", [P, RAW, 2048])
        w_hi = sb("w_hi", [P, RING, 2048], f32r)
        w_lo = sb("w_lo", [P, RING, 2048], f32r)
        x = sb("x", [P, TB, D])
        xn = sb("xn", [P, TB, D])
        at_h = sb("at_h", [P, KT, S], f32r)
        at_l = sb("at_l", [P, KT, S], f32r)
        mem_h = sb("mem_h", [P, KT, S], f32r)
        mem_l = sb("mem_l", [P, KT, S], f32r)
        hid_h = sb("hid_h", [P, 3, 2 * S], f32r)
        hid_l = sb("hid_l", [P, 3, 2 * S], f32r)
        gain = sb("gain", [P, 2, D])
        ident = sb("ident", [P, P])
        zeros = sb("zeros", [P, 512], bf16)
        stat = sb("stat", [P, 8, 2 * N_NORMS])
        eps = sb("eps", [P, 3])
        arena = sb("arena", [P, 15872])
        Y = ctx.enter_context(nc.psum_tensor("Y", [P, 4, 512], f32))
        C = ctx.enter_context(nc.psum_tensor("C", [P, 4, 512], f32))
        used = [0]

        def room(cols, start=None):
            at = used[0] if start is None else start
            used[0] = at + cols
            assert used[0] <= 15872
            return arena[:, at:at + cols]

        def tiles(ap, n):
            return ap.rearrange("p (a b) -> p a b", a=n)

        room(0, 0)
        u_t, f_t, v_t, g_t = (tiles(room(TB * 512), TB) for _ in range(4))
        q_d, k_d = (tiles(room(4 * S), 4) for _ in range(2))
        fall = [room(4 * S) for _ in range(2)]
        both = [tiles(room(4 * S), 4) for _ in range(2)]
        scores = room(3 * 4 * P)
        score = [tiles(scores[:, i * 4 * P:(i + 1) * 4 * P], 4) for i in range(3)]
        span_c = room(len(LEVELS) * P)
        pair_c = room(len(LEVELS) * P)
        after_c = room(P)
        upto_c = room(P)
        lb = room(512)
        not_lb = room(512)
        og = room(P)
        pscale = room(4)
        h_stat = tiles(room(8 * 8), 8)
        pool_w = tiles(room(4 * P), 4)
        flat = "p a b -> p (a b)"
        pool_c = [both[0].rearrange(flat), fall[0]]
        pooled = both[1]
        mem_x = tiles(arena[:, 4 * TB * 512:4 * TB * 512 + TB * D], TB)
        exp_f = k_d.rearrange(flat)
        soft_f = fall[1]
        key = scores[:, 0:TB * 512]
        room(0, 0)
        qT, kT = (tiles(room(8 * S), 8) for _ in range(2))
        vt = tiles(room(TB * D), TB)
        SEEN = 3 * P
        sc = [room(2 * S) for _ in range(2)]
        pr = [room(2 * S) for _ in range(3)]
        pT = [room(2 * S) for _ in range(3)]
        bias = [room(2 * S) for _ in range(2)]
        mask = room(SEEN)
        a_stat = tiles(room(5 * 32), 5)
        sinks = room(32)
        after_s, ones_s, flip_c = (room(P) for _ in range(3))
        rope_at = used[0]
        rope = tiles(room(2 * S), 2)
        turn_c, low_c, high_c = (room(P) for _ in range(3))
        rot = [room(2 * S) for _ in range(2)]
        kdup = tiles(room(4 * S), 4)
        mem_kT = tiles(room(8 * S, rope_at), 8)
        relu = sc + bias[:1]
        full = pr

        loaded = [sem(f"loaded{i}") for i in range(RAW)]
        hi_split = sem("hi_split")
        lo_split = sem("lo_split")
        chunk_done = sem("chunk_done")
        cols_copied = sem("cols_copied")
        up_used = sem("up_used")
        y_ready = sem("y_ready")
        squared = sem("squared")
        guessed = sem("guessed")
        x_ready = sem("x_ready")
        xn_ready = sem("xn_ready")
        xt_ready = sem("xt_ready")
        at_hi = sem("at_hi")
        at_lo = sem("at_lo")
        first_gain_in = sem("first_gain_in")
        gains_in = [sem(f"gains_in{i}") for i in range(2)]
        hid_hi = sem("hid_hi")
        hid_lo = sem("hid_lo")
        act_seq = sem("act_seq")
        dve_seq = sem("dve_seq")
        tokens_in = [sem(f"tokens_in{b}") for b in range(TB)]
        mem_in, ident_in = sem("mem_in"), sem("ident_in")
        setup = sem("setup")
        out_done = sem("out_done")
        lb_in, even_in, pool_in = sem("lb_in"), sem("even_in"), sem("pool_in")
        band_in, stick_in, swa_in = sem("band_in"), sem("stick_in"), sem("swa_in")
        bias_in = [sem(f"bias_in{i}") for i in range(2)]
        lb_shifted, lb_exp = sem("lb_shifted"), sem("lb_exp")
        clipped, gates_exp, lb_scaled = sem("clipped"), sem("gates_exp"), sem("lb_scaled")
        gates_ln, keys_ready, decays_ready = sem("gates_ln"), sem("keys_ready"), sem("decays_ready")
        keys_shared, keys_exp = sem("keys_shared"), sem("keys_exp")
        keys_turned, keys_copied = sem("keys_turned"), sem("keys_copied")
        gated = sem("gated")
        pool_ready, pool_copied = sem("pool_ready"), sem("pool_copied")
        mix_ready, mix_hi, mix_lo = sem("mix_ready"), sem("mix_hi"), sem("mix_lo")
        level_sum, level_exp, level_both = sem("level_sum"), sem("level_exp"), sem("level_both")
        level_score, level_used = sem("level_score"), sem("level_used")
        rec_ready, rec_squared, rec_meaned = sem("rec_ready"), sem("rec_squared"), sem("rec_meaned")
        rec_guessed, rec_normed, rec_turned = sem("rec_guessed"), sem("rec_normed"), sem("rec_turned")
        rec_hi, rec_lo = sem("rec_hi"), sem("rec_lo")
        scores_ready = sem("scores_ready")
        scores_scaled = sem("scores_scaled")
        scores_max = sem("scores_max")
        probs_ready = sem("probs_ready")
        probs_scaled = sem("probs_scaled")
        probs_turned = sem("probs_turned")
        probs_copied = sem("probs_copied")
        probs_used = sem("probs_used")
        sink_ready = sem("sink_ready")
        ctx_hi, ctx_lo = sem("ctx_hi"), sem("ctx_lo")
        turned, rotated = sem("turned"), sem("rotated")
        kdup_ready, kdup_copied = sem("kdup_ready"), sem("kdup_copied")
        z_ready = sem("z_ready")
        soft_ready = sem("soft_ready")
        keep_ready = sem("keep_ready")
        keep_masked = sem("keep_masked")
        suffix_ready = sem("suffix_ready")
        suffix_added = sem("suffix_added")
        weights_ready = sem("weights_ready")
        weights_masked = sem("weights_masked")
        weights_used = sem("weights_used")

        def weight(name, l):
            return a[name] if l is None else a[name][l]

        def col(name, l, c, off=0):
            first = c * CH + off
            return weight(name, l).rearrange("(k p) n -> p k n", p=P)[:, :, bass.ds(first, CH)]

        def row(name, l, r, off=0):
            return weight(name, l)[bass.ds(r * CH + off, CH), :].rearrange("(k p) n -> p k n", p=P)

        even_cols = [("w_in_ab", 0, c, "T" if c in (2, 3) else "N", "at") for c in (8, 9, 4, 5, 0, 1, 2, 3, 6, 7)]
        qkv_cols = [("w_qkv", 0, c, "TTN"[c // 4], "at") for c in range(12)]
        stick_cols = [("sb_w_qkv_2", 0, c, "TTN"[c // 4], "at") for c in (8, 9, 10, 11, 0, 1, 2, 3, 4, 5, 6, 7)]
        kv_cols = [("kv_w_2", None, 1, "N", "at"), ("kv_w_2", None, 0, "T", "at")]
        q_cols = [("swa_w_q_2", 0, c, "T", "at") for c in range(4)]

        def mem_q(l):
            return [("w_mem_q", l, c, "T", "at") for c in range(4)]

        def mem_k(l):
            return [("w_mem_kv", l, c, "T", "mem") for c in range(4)]

        def mem_v(l):
            return [("w_mem_kv", l, 4 + c, "N", "mem") for c in range(4)]

        def halves(t, c):
            return t[:, 2 * c:2 * c + 2, :]

        def wide(t, c):
            return t[:, :, c * CH:(c + 1) * CH]

        even_to = [wide(g_t, 0), wide(g_t, 1), wide(f_t, 0), wide(f_t, 1), wide(u_t, 0), wide(u_t, 1),
                   halves(q_d, 0), halves(q_d, 1), wide(v_t, 0), wide(v_t, 1)]
        qkv_to = [halves(qT, c) for c in range(4)] + [halves(kT, c) for c in range(4)] + [wide(vt, c) for c in range(4)]
        stick_to = qkv_to[8:] + qkv_to[:8]
        kv_to = [wide(vt, 0), halves(kT, 0)]
        q_to = [halves(qT, c) for c in range(4)]
        mem_k_to = [halves(mem_kT, c) for c in range(4)]
        v_to = [wide(vt, c) for c in range(4)]

        ng = a["norm_gains"]
        gain_rows = [ng[0, 0], a["mem_norm_gain"], *(ng[0, i] for i in range(1, 6)), *(ng[1, i] for i in range(6)),
                     a["ffn1_norm_2"][0], a["mix_norm_2"][0], a["ffn2_norm_2"][0], a["kv_norm_2"],
                     a["ffn1_norm_2"][1], a["mix_norm_2"][1], a["ffn2_norm_2"][1], a["final_norm_2"]]

        net = [("norm", "at"), ("even_cols", even_cols, even_to), ("even",), ("rows", "w_out_ab", 0),
               ("meanwhile", mem_k(0) + mem_v(0), mem_k_to + v_to)]
        for l in range(2):
            if l == 1:
                net += [("meanwhile", mem_k(1), mem_k_to), ("cols", qkv_cols, qkv_to), ("softmax", "band", 16),
                        ("rows", "w_o_att", 0), ("meanwhile", mem_v(1), v_to)]
            net += [("cols", mem_q(l), q_to), ("softmax", "mem", 4), ("rows", "w_mem_o", l),
                    ("post",), ("norm", "at"), ("relu_ff", l)]
        net += [("post",), ("norm", "at")]
        for l in range(2):
            net += [("swiglu", "ffn1", l), ("add", 0.5)]
            if l == 0:
                net += [("norm", "at"), ("cols", stick_cols, stick_to), ("stick",), ("rows", "sb_w_o_2", 0)]
            else:
                net += [("norm", "at", "double"), ("q_cols", q_cols, q_to), ("softmax", "swa", 16),
                        ("rows", "swa_w_o_2", 0)]
            net += [("add", 1.0), ("norm", "at"), ("swiglu", "ffn2", l), ("add", 0.5)]
            if l == 0:
                net += [("norm", "at"), ("kv_cols", kv_cols, kv_to), ("norm", "same")]
        net += [("norm", "out")]

        N_REL, N_GLU = FF // CH, DFF // CH

        def counts(s):
            if s[0] == "norm":
                return dict(norm=1, rms=s[1] != "same", xn=2, turned=4 * (s[1] != "out"))
            if s[0] == "post":
                return dict(norm=1, rms=1, x=2)
            if s[0] == "meanwhile":
                return dict(norm=2, rms=2, x=2, xn=2, turned=4, chunk=len(s[1]), copied=len(s[1]))
            if s[0] == "add":
                return dict(x=2)
            if s[0] == "cols":
                return dict(chunk=len(s[1]), copied=len(s[1]))
            if s[0] == "even_cols":
                return dict(norm=1, rms=1, xn=2, turned=4, chunk=len(s[1]), copied=len(s[1]))
            if s[0] == "rows":
                return dict(chunk=4, y=1)
            if s[0] == "relu_ff":
                return dict(chunk=2 * N_REL, y=1, copied=N_REL, hid=N_REL, hid_hi=N_REL)
            if s[0] == "swiglu":
                return dict(chunk=3 * N_GLU, y=1, copied=N_GLU, up=N_GLU, hid=N_GLU)
            if s[0] == "softmax":
                return dict(head=s[2], ctx=4 if s[1] == "mem" else 8)
            if s[0] == "stick":
                return dict(ctx=8)
            if s[0] == "kv_cols":
                return dict(chunk=len(s[1]), copied=len(s[1]), rot=1)
            if s[0] == "q_cols":
                return dict(chunk=len(s[1]), copied=len(s[1]), rot=len(s[1]))
            return {}

        before, so_far = [], dict(norm=0, rms=0, xn=0, turned=0, x=0, y=0, chunk=0, copied=0, hid=0,
                                  hid_hi=0, up=0, head=0, ctx=0, rot=0)
        for s in net:
            before.append((s, Counts(**so_far)))
            for k, v in counts(s).items():
                so_far[k] += v
        N_CHUNKS = so_far["chunk"]

        def glu_turns(n):
            return (N_GLU - 1) // 2 - (n + 3 * N_GLU == N_CHUNKS)

        gain_done = []
        for s, at in before:
            if s[0] in ("post", "meanwhile"):
                gain_done.append((x_ready, at.x + TB))
            if s[0] in ("norm", "even_cols", "meanwhile"):
                gain_done.append((xn_ready, at.xn + TB))

        def behind_post(at):
            return Counts(at.norm + 1, at.rms + 1, at.xn, at.turned, at.x + 2, at.y, at.chunk, at.copied, at.hid,
                          at.hid_hi, at.up, at.head, at.ctx, at.rot)

        def rows_of(kind):
            return ((0, S), (S, 2 * S)) if kind == "mem" else ((0, P), (P, SEEN))

        block = ctx.enter_context(nc.Block())

        @block.sync
        def _(sp):
            def load(src, slot, at, first=False):
                if not first:
                    sp.wait_ge(lo_split, at - RAW + 1)
                sp.dma_start(raw[:, slot, :].rearrange("p (k n) -> p k n", k=src.shape[1]), src) \
                    .then_inc(loaded[slot], 16)

            for b in range(TB):
                sp.dma_start(x[:, b, :], a["x"][0, b * P:(b + 1) * P, :]).then_inc(tokens_in[b], 16)
            sp.dma_start(gain[:, 0, :], gain_rows[0].partition_broadcast(P)).then_inc(first_gain_in, 16)
            for s, at in before:
                n = at.chunk
                if s[0] in ("cols", "even_cols", "q_cols", "kv_cols", "meanwhile"):
                    for i, (name, l, c, _, _) in enumerate(s[1]):
                        load(col(name, l, c), (n + i) % RAW, n + i, n + i < RAW)
                        if s[0] == "even_cols" and i == RAW:
                            sp.dma_start(mem_x, a["mem"][0].rearrange("(b p) d -> p b d", p=P)).then_inc(mem_in, 16)
                elif s[0] == "rows":
                    for r in range(4):
                        load(row(s[1], s[2], r), (n + r) % RAW, n + r)
                elif s[0] == "relu_ff":
                    l, end = s[1], n + 2 * N_REL - 1
                    load(col("w_ff1", l, 0), n % RAW, n)
                    with nc.sync.Fori(0, (N_REL - 1) // 3) as t:
                        for j in range(3):
                            up, down = n + 1 + 2 * j, n + 2 + 2 * j
                            load(col("w_ff1", l, j + 1, t * (3 * CH)), up % RAW, t * 6 + up)
                            load(row("w_ff2", l, j, t * (3 * CH)), down % RAW, t * 6 + down)
                    load(row("w_ff2", l, N_REL - 1), end % RAW, end)
                elif s[0] == "swiglu":
                    wi, wo, l, end = s[1] + "_w_in_2", s[1] + "_w_out_2", s[2], n + 3 * N_GLU - 1
                    load(col(wi, l, 0), n % RAW, n)
                    load(col(wi, l, N_GLU), (n + 1) % RAW, n + 1)
                    with nc.sync.Fori(0, (N_GLU - 1) // 2) as t:
                        for j in range(2):
                            gate = n + 2 + 3 * j
                            load(col(wi, l, j + 1, t * (2 * CH)), gate % RAW, t * 6 + gate)
                            load(col(wi, l, N_GLU + j + 1, t * (2 * CH)), (gate + 1) % RAW, t * 6 + (gate + 1))
                            load(row(wo, l, j, t * (2 * CH)), (gate + 2) % RAW, t * 6 + (gate + 2))
                    load(row(wo, l, N_GLU - 1), end % RAW, end)
                elif s == ("norm", "out"):
                    for b in range(TB):
                        sp.wait_ge(xn_ready, at.xn + b + 1)
                        sp.dma_start(out[0, b * P:(b + 1) * P, :], xn[:, b, :]).then_inc(out_done, 16)
            sp.wait_ge(out_done, 16 * TB)

        @block.gpsimd
        def _(pool):
            for i, factor in enumerate((1, 4, -4)):
                nc.gpsimd.memset(eps[:, i:i + 1], factor * EPS)
            nc.gpsimd.memset(zeros[:], 0.0).then_inc(setup, 1)
            pool.dma_start(ident[:], a["ident"]).then_inc(ident_in, 16)
            for s, at in before:
                if s[0] in ("norm", "post", "even_cols", "meanwhile") and at.norm > 0:
                    for i in range(at.norm, at.norm + (2 if s[0] == "meanwhile" else 1)):
                        if i >= 2:
                            pool.wait_ge(*gain_done[i - 2])
                        pool.dma_start(gain[:, i % 2, :], gain_rows[i].partition_broadcast(P)).then_inc(gains_in[i % 2], 16)
                if s[0] == "even_cols":
                    pool.dma_start(lb, a["rec_lb_logits"][0].partition_broadcast(P)).then_inc(lb_in, 16)
                    pool.wait_ge(chunk_done, at.chunk + 2)
                    for i in range(2):
                        pool.dma_start(pool_c[i], a["pool"][:, i * 4 * S:(i + 1) * 4 * S]).then_inc(pool_in, 16)
                    pool.wait_ge(chunk_done, at.chunk + 4)
                    for to, src in ((og, a["rec_out_gain"][0].partition_broadcast(P)),
                                    (pool_w, a["pool_w"][0].rearrange("g c d -> c g d")),
                                    (pscale, a["pool_scale_by_group"]), (after_c, a["after"]), (upto_c, a["upto"]),
                                    (span_c, a["span"]), (pair_c, a["pair"])):
                        pool.dma_start(to, src).then_inc(even_in, 16)
                elif s[0] == "cols" and s[1] is qkv_cols:
                    pool.wait_ge(x_ready, at.x)
                    pool.dma_start(mask, a["band"]).then_inc(band_in, 16)
                    pool.dma_start(flip_c, a["flip"]).then_inc(band_in, 16)
                elif s[0] == "cols" and s[1] is stick_cols:
                    pool.wait_ge(x_ready, at.x)
                    for to, src in ((mask[:, 0:P], a["strict"]), (after_s, a["after"]), (ones_s, a["ones"])):
                        pool.dma_start(to, src).then_inc(stick_in, 16)
                elif s[0] == "kv_cols":
                    pool.wait_ge(x_ready, at.x)
                    for to, src in ((rope[:, 0, :], a["cos"]), (rope[:, 1, :], a["sin"]), (turn_c, a["turn"]),
                                    (low_c, a["low"]), (high_c, a["high"]), (mask, a["swa"]),
                                    (sinks[:, 0:16], a["swa_sinks_2"][0].partition_broadcast(P))):
                        pool.dma_start(to, src).then_inc(swa_in, 16)
                elif s[0] == "softmax" and s[1] == "band":
                    table = a["rel_reversed"]
                    for p in range(8):
                        if p >= 2:
                            pool.wait_ge(scores_ready, at.head + 2 * p - 2)
                        src = bass.AP(table.tensor, 2 * p * (2 * REL + 1) + REL - S + 1, [[1, P], [2 * REL + 1, 2], [1, S]])
                        pool.dma_start(tiles(bias[p % 2], 2), src).then_inc(bias_in[p % 2], 16)
                elif s[0] == "stick":
                    pool.wait_ge(stick_in, 48)
                    strict = mask[:, None, 0:P].broadcast_to([P, 2, P])
                    for i in range(16 + 2):
                        if i < 16:
                            pool.wait_ge(keep_ready, i + 1)
                            own = tiles(pr[i % 2][:, 0:SEEN], 3)[:, 0:3:2, :]
                            nc.gpsimd.tensor_tensor(own, own, strict, ALU.mult).then_inc(keep_masked, 1)
                        if i >= 2:
                            pool.wait_ge(weights_ready, i - 1)
                            own = tiles(pT[(i - 2) % 3][:, 0:SEEN], 3)[:, 0:3:2, :]
                            nc.gpsimd.tensor_tensor(own, own, strict, ALU.mult).then_inc(weights_masked, 1)

        @block.scalar
        def _(act):
            seq = [0]

            def again(ins):
                seq[0] += 1
                ins.then_inc(act_seq, 1)
                act.wait_ge(act_seq, seq[0])

            def exp_and_ln():
                nc.scalar.preload_act_table_set("natural_log_exp_and_others")

            def hi(n, t=None):
                if n >= N_CHUNKS:
                    return
                step = (lambda k, v: v) if t is None else (lambda k, v: t * k + v)
                act.wait_ge(loaded[n % RAW], step(6 // RAW * 16, 16 * (n // RAW + 1)))
                if n >= RING:
                    act.wait_ge(chunk_done, step(6, n - RING + 1))
                nc.scalar.activation(w_hi[:, n % RING, :], raw[:, n % RAW, :], ACT.Copy).then_inc(hi_split, 1)

            def guess(src, b, at):
                j = 2 * at.rms + b
                nc.scalar.activation(xn[:, b, :], src, ACT.Square, accum_out=stat[:, 0, j:j + 1]).then_inc(squared, 1)
                act.wait_ge(squared, j + 1)
                ln = nc.scalar.activation(stat[:, 1, j:j + 1], stat[:, 0, j:j + 1], ACT.Ln, bias=eps[:, 1:2], scale=4.0 / D)
                nc.scalar.activation(stat[:, 3, j:j + 1], stat[:, 0, j:j + 1], ACT.Identity, bias=eps[:, 2:3], scale=-4.0 / D)
                again(ln)
                nc.scalar.activation(stat[:, 2, j:j + 1], stat[:, 1, j:j + 1], ACT.Exp, scale=-0.5).then_inc(guessed, 1)

            def norm_guess(to, at):
                for b in range(TB):
                    if to == "mem":
                        act.wait_ge(mem_in, 16)
                    elif at.x == 0:
                        act.wait_ge(tokens_in[b], 16)
                    else:
                        act.wait_ge(x_ready, at.x - 1 + b)
                    guess(mem_x[:, b, :] if to == "mem" else x[:, b, :], b, at)

            def norm_hi(to, at, banks):
                for b in range(TB):
                    for h in range(2):
                        act.wait_ge(xt_ready, at.turned + 2 * b + h + 1)
                        nc.scalar.activation((mem_h if to == "mem" else at_h)[:, 4 * h:4 * h + 4, b * P:(b + 1) * P],
                                             tiles(banks[:, 2 * b + h, :], 4), ACT.Copy).then_inc(at_hi, 1)

            def norm(to, at, double):
                if to != "same":
                    norm_guess(to, at)
                if double:
                    act.wait_ge(kdup_ready, 1)
                    nc.scalar.activation(kdup, C[:, 2:4, :].rearrange("p a (b c) -> p (a b) c", b=2), ACT.Copy) \
                        .then_inc(kdup_copied, 1)
                if to == "out":
                    return
                if at.chunk == 0:
                    hi(0)
                norm_hi(to, at, C)
                if at.chunk == 0:
                    for n in range(1, AHEAD):
                        hi(n)

            def post(at):
                for b in range(TB):
                    if b == 0:
                        act.wait_ge(y_ready, at.y)
                    else:
                        act.wait_ge(chunk_done, at.chunk)
                    guess(Y[:, 2 * b:2 * b + 2, :], b, at)

            def copied(i, specs, to, at):
                act.wait_ge(chunk_done, at.chunk + i + 1)
                f = ACT.Silu if specs is even_cols and i < 2 else ACT.Copy
                size = 64 ** -0.5 if specs is stick_cols and specs[i][2] < 4 else 1.0
                nc.scalar.activation(to[i], tiles(C[:, i % 4, :], 2), f, scale=size).then_inc(cols_copied, 1)

            def meanwhile(specs, to, at):
                then = behind_post(at)
                post(at)
                for i in range(len(specs)):
                    hi(at.chunk + i + AHEAD)
                    if i == len(specs) - 1:
                        norm_hi("at", then, Y)
                    copied(i, specs, to, at)
                    if i == 0:
                        norm_guess("at", then)

            def cols(specs, to, at):
                for i in range(len(specs)):
                    hi(at.chunk + i + AHEAD)
                    copied(i, specs, to, at)

            def rows(at, first):
                for i in range(first, 4):
                    hi(at.chunk + i + AHEAD)

            def relu_ff(at):
                n = at.chunk

                def units(j, t=None):
                    step = (lambda v: v) if t is None else (lambda v: t * 3 + v)
                    up = n if j == 0 else n + 2 * j - 1
                    act.wait_ge(chunk_done, up + 1 if t is None else t * 6 + (up + 1))
                    nc.scalar.activation(relu[j % 3], C[:, j % 3, :], ACT.Relu).then_inc(cols_copied, 1)
                    act.wait_ge(cols_copied, step(at.copied + j + 1))
                    nc.scalar.activation(full[j % 3], relu[j % 3], ACT.Square)
                    nc.scalar.activation(hid_h[:, j % 3, :], relu[j % 3], ACT.Square).then_inc(hid_hi, 1)

                hi(n + AHEAD)
                units(0)
                with nc.scalar.Fori(0, (N_REL - 1) // 3) as t:
                    for j in range(3):
                        hi(n + 1 + 2 * j + AHEAD, t)
                        units(j + 1, t)
                        hi(n + 2 + 2 * j + AHEAD, t)
                hi(n + 2 * N_REL - 1 + AHEAD)

            def swiglu(at):
                n = at.chunk

                def gate(j, t=None):
                    step = (lambda k, v: v) if t is None else (lambda k, v: t * k + v)
                    act.wait_ge(chunk_done, step(6, (n if j == 0 else n + 3 * j - 1) + 1))
                    nc.scalar.activation(relu[j % 2], C[:, 2 * (j % 2), :], ACT.Silu).then_inc(cols_copied, 1)

                hi(n + AHEAD)
                gate(0)
                hi(n + 1 + AHEAD)

                def three(j, t=None):
                    b = n + 2 + 3 * j + AHEAD
                    hi(b, t)
                    gate(j + 1, t)
                    hi(b + 1, t)
                    hi(b + 2, t)

                turns = glu_turns(n)
                with nc.scalar.Fori(0, turns) as t:
                    for j in range(2):
                        three(j, t)
                for j in range(2 * turns, N_GLU - 1):
                    three(j)
                hi(n + 3 * N_GLU - 1 + AHEAD)

            def contexts(i, at, kind):
                if kind == "stick":
                    act.wait_ge(weights_used, 2 * i + 2)
                else:
                    act.wait_ge(probs_used, at.head + (i + 1 if kind == "mem" else 2 * i + 2))
                if kind == "mem":
                    nc.scalar.activation(at_h[:, 2 * i:2 * i + 2, :], tiles(Y[:, i % 2, :], 2), ACT.Copy).then_inc(ctx_hi, 1)
                else:
                    nc.scalar.activation(at_h[:, i, :], Y[:, i % 2, 0:S], ACT.Copy).then_inc(ctx_hi, 1)

            def softmax(kind, heads, at):
                h0 = at.head
                for i in range(heads + 4):
                    if i < heads:
                        act.wait_ge(scores_max, h0 + i + 1)
                        if i >= 3:
                            act.wait_ge(probs_turned, h0 + i - 2)
                        for b, (first, end) in enumerate(rows_of(kind)):
                            j = 2 * i + b
                            src, size = (C[:, i % 2, :], 0.0625) if kind == "mem" else (sc[i % 2], 1.0)
                            last = nc.scalar.activation(pr[i % 3][:, first:end], src[:, first:end], ACT.Exp,
                                                        bias=a_stat[:, 0, j:j + 1], scale=size, accum_out=a_stat[:, 1, j:j + 1])
                        if kind == "swa":
                            last = nc.scalar.activation(a_stat[:, 3, 2 * i:2 * i + 2], a_stat[:, 0, 2 * i:2 * i + 2], ACT.Exp,
                                                        bias=sinks[:, i:i + 1])
                        last.then_inc(probs_ready, 1)
                    if 2 <= i < heads + 2:
                        k = i - 2
                        act.wait_ge(probs_turned, h0 + k + 1)
                        if k >= 2:
                            act.wait_ge(probs_used, h0 + k - 1)
                        width = rows_of(kind)[-1][1]
                        nc.scalar.activation(pT[k % 2][:, 0:width], C[:, 2 + k % 2, 0:width], ACT.Copy).then_inc(probs_copied, 1)
                    if i >= 3 and (kind == "mem" or i % 2 == 0) and i - 3 < heads:
                        contexts(i - 3 if kind == "mem" else (i - 3) // 2, at, kind)

            def stick(at):
                for i in range(16 + 5):
                    if i < 16:
                        act.wait_ge(z_ready, i + 1)
                        if i >= 2:
                            act.wait_ge(keep_ready, i - 1)
                        soft = sc[i % 2][:, 0:SEEN]
                        again(nc.scalar.activation(soft, C[:, i % 2, 0:SEEN], ACT.Abs))
                        again(nc.scalar.activation(soft, soft, ACT.Exp, scale=-1.0))
                        nc.scalar.activation(soft, soft, ACT.Ln, bias=1.0).then_inc(soft_ready, 1)
                    if 3 <= i < 16 + 3:
                        w = pT[(i - 3) % 3][:, 0:SEEN]
                        act.wait_ge(suffix_added, i - 2)
                        nc.scalar.activation(w, w, ACT.Exp).then_inc(weights_ready, 1)
                    if i >= 5 and i % 2 == 1:
                        contexts((i - 5) // 2, at, "stick")

            def even_cols_(specs, to, at):
                f = f_t.rearrange(flat)
                for i in range(len(specs)):
                    hi(at.chunk + i + AHEAD)
                    copied(i, specs, to, at)
                    if i == 1:
                        exp_and_ln()
                        act.wait_ge(lb_shifted, 1)
                        nc.scalar.activation(not_lb, lb, ACT.Exp).then_inc(lb_exp, 1)
                        norm_guess("mem", at)
                    elif i == 3:
                        act.wait_ge(clipped, 1)
                        again(nc.scalar.activation(soft_f, f, ACT.Abs))
                        again(nc.scalar.activation(soft_f, soft_f, ACT.Exp, scale=-1.0))
                    elif i == 4:
                        norm_hi("mem", at, Y)
                    elif i == 5:
                        nc.scalar.activation(soft_f, soft_f, ACT.Ln, bias=1.0)
                        nc.scalar.activation(exp_f, f, ACT.Exp, scale=-1.0).then_inc(gates_exp, 1)
                    elif i == 7:
                        act.wait_ge(keys_shared, 1)
                        nc.scalar.activation(key, key, ACT.Exp).then_inc(keys_exp, 1)
                        act.wait_ge(pool_ready, 1)
                        nc.scalar.activation(pooled, Y[:, 2:4, :].rearrange("p a (b c) -> p (a b) c", b=2), ACT.Copy) \
                            .then_inc(pool_copied, 1)
                    elif i == 8:
                        act.wait_ge(lb_scaled, 1)
                        nc.scalar.activation(xn[:, 0, :], xn[:, 0, :], ACT.Ln, bias=1.0).then_inc(gates_ln, 1)
                        act.wait_ge(keys_turned, 1)
                        for b in range(TB):
                            last = nc.scalar.activation(k_d[:, :, b * P:(b + 1) * P], tiles(Y[:, b, :], 4), ACT.Copy)
                        last.then_inc(keys_copied, 1)

            def even(at):
                act.wait_ge(mix_ready, 1)
                for g in range(4):
                    last = nc.scalar.activation(at_h[:, g, :], Y[:, 2 + g // 2, g % 2 * S:(g % 2 + 1) * S], ACT.Copy,
                                                scale=pscale[:, g:g + 1])
                last.then_inc(mix_hi, 1)
                for l in range(1 + len(LEVELS)):
                    act.wait_ge(level_sum, l + 1)
                    if l >= 2:
                        act.wait_ge(level_both, l - 1)
                    bank = 2 * (l % 2)
                    nc.scalar.activation(tiles(fall[l % 2], 2), Y[:, bank:bank + 2, :], ACT.Exp).then_inc(level_exp, 1)
                act.wait_ge(rec_ready, 1)
                for b in range(TB):
                    last = nc.scalar.activation(xn[:, b, 512:1024], C[:, 2 + b, :], ACT.Square)
                last.then_inc(rec_squared, 1)
                act.wait_ge(rec_meaned, 1)
                again(nc.scalar.activation(h_stat[:, 1, :], h_stat[:, 0, :], ACT.Ln, bias=eps[:, 0:1], scale=1.0 / P))
                nc.scalar.activation(h_stat[:, 2, :], h_stat[:, 1, :], ACT.Exp, scale=-0.5).then_inc(rec_guessed, 1)
                hi(at.chunk + AHEAD)
                for b in range(TB):
                    act.wait_ge(rec_turned, b + 1)
                    nc.scalar.activation(at_h[:, 4:8, b * P:(b + 1) * P], tiles(C[:, b, :], 4), ACT.Copy).then_inc(rec_hi, 1)
                hi(at.chunk + 1 + AHEAD)

            act.wait_ge(setup, 1)
            exp_and_ln()
            for s, at in before:
                if s[0] == "norm":
                    norm(s[1], at, len(s) > 2)
                elif s[0] == "post":
                    post(at)
                elif s[0] in ("cols", "q_cols", "kv_cols"):
                    cols(s[1], s[2], at)
                elif s[0] == "even_cols":
                    even_cols_(s[1], s[2], at)
                elif s[0] == "rows":
                    rows(at, 2 if s[1] == "w_out_ab" else 0)
                elif s[0] == "relu_ff":
                    relu_ff(at)
                elif s[0] == "swiglu":
                    swiglu(at)
                    exp_and_ln()
                elif s[0] == "softmax":
                    softmax(s[1], s[2], at)
                elif s[0] == "meanwhile":
                    meanwhile(s[1], s[2], at)
                elif s[0] == "stick":
                    stick(at)
                elif s[0] == "even":
                    even(at)

        @block.vector
        def _(dve):
            V = nc.vector
            seq = [0]

            def again(ins):
                seq[0] += 1
                ins.then_inc(dve_seq, 1)
                dve.wait_ge(dve_seq, seq[0])

            def lo(n, t=None):
                if n >= N_CHUNKS:
                    return
                dve.wait_ge(hi_split, n + 1 if t is None else t * 6 + (n + 1))
                V.tensor_tensor(w_lo[:, n % RING, :], raw[:, n % RAW, :], w_hi[:, n % RING, :].bitcast(f32),
                                ALU.subtract).then_inc(lo_split, 1)

            def newton(guess, mean, scratch):
                again(V.tensor_tensor(scratch[0], guess, guess, ALU.mult))
                again(V.tensor_tensor(scratch[0], scratch[0], mean, ALU.mult))
                again(V.tensor_scalar(scratch[1], scratch[0], -0.5, 1.5, ALU.mult, ALU.add))
                again(V.tensor_tensor(scratch[2], guess, scratch[1], ALU.mult))

            def rms(b, at):
                j = 2 * at.rms + b
                guess, v4, part, r = (stat[:, k, j:j + 1] for k in (2, 3, 4, 6))
                dve.wait_ge(guessed, j + 1)
                again(V.scalar_tensor_tensor(part, guess, v4, guess, ALU.mult, ALU.mult))
                again(V.scalar_tensor_tensor(r, part, 3.0, guess, ALU.add, ALU.mult))

            def scaled(src, b, at, same=False):
                j = 2 * at.rms + b
                if same:
                    j -= 2
                else:
                    rms(b, at)
                if at.norm == 0:
                    dve.wait_ge(first_gain_in, 16)
                else:
                    dve.wait_ge(gains_in[at.norm % 2], 16 * ((at.norm + 1) // 2))
                return V.scalar_tensor_tensor(xn[:, b, :], src, stat[:, 6, j:j + 1], gain[:, at.norm % 2, :], ALU.mult, ALU.mult)

            def norm_scale(to, at):
                for b in range(TB):
                    src = mem_x[:, b, :] if to == "mem" else x[:, b, :]
                    scaled(src, b, at, to == "same").then_inc(xn_ready, 1)

            def norm_lo(to, at, banks):
                h, l = (mem_h, mem_l) if to == "mem" else (at_h, at_l)
                for b in range(TB):
                    for k in range(2):
                        dve.wait_ge(at_hi, at.turned + 2 * b + k + 1)
                        part = (slice(None), slice(4 * k, 4 * k + 4), slice(b * P, (b + 1) * P))
                        V.tensor_tensor(l[part], tiles(banks[:, 2 * b + k, :], 4), h[part].bitcast(f32),
                                        ALU.subtract).then_inc(at_lo, 1)

            def norm(to, at):
                norm_scale(to, at)
                if to == "out":
                    return
                if at.chunk == 0:
                    lo(0)
                norm_lo(to, at, C)
                if at.chunk == 0:
                    for n in range(1, AHEAD):
                        lo(n)
                elif to == "at":
                    lo(at.chunk - 1 + AHEAD)
                else:
                    rope_keys(at)

            def post(at):
                for b in range(TB):
                    again(scaled(Y[:, 2 * b:2 * b + 2, :].rearrange(flat), b, at))
                    V.tensor_tensor(x[:, b, :], x[:, b, :], xn[:, b, :], ALU.add).then_inc(x_ready, 1)

            def meanwhile(n, at):
                then = behind_post(at)
                lo(at.chunk - 1 + AHEAD)
                post(at)
                for i in range(n):
                    lo(at.chunk + i + AHEAD)
                    if i == 0:
                        norm_scale("at", then)
                    if i == n - 1:
                        norm_lo("at", then, Y)

            def add(factor, at):
                for b in range(TB):
                    if b == 0:
                        dve.wait_ge(y_ready, at.y)
                    else:
                        dve.wait_ge(chunk_done, at.chunk)
                    V.scalar_tensor_tensor(x[:, b, :], Y[:, 2 * b:2 * b + 2, :].rearrange(flat), factor, x[:, b, :],
                                           ALU.mult, ALU.add).then_inc(x_ready, 1)

            def cols(first, n, at):
                for i in range(first, n):
                    lo(at.chunk + i + AHEAD)

            def relu_ff(at):
                n = at.chunk

                def units(j, t=None):
                    dve.wait_ge(hid_hi, at.hid_hi + j + 1 if t is None else t * 3 + (at.hid_hi + j + 1))
                    V.tensor_tensor(hid_l[:, j % 3, :], full[j % 3], hid_h[:, j % 3, :].bitcast(f32),
                                    ALU.subtract).then_inc(hid_lo, 1)

                lo(n + AHEAD)
                units(0)
                with nc.vector.Fori(0, (N_REL - 1) // 3) as t:
                    for j in range(3):
                        lo(n + 1 + 2 * j + AHEAD, t)
                        units(j + 1, t)
                        lo(n + 2 + 2 * j + AHEAD, t)

            def swiglu(at):
                n = at.chunk

                def units(j, t=None):
                    step = (lambda k, v: v) if t is None else (lambda k, v: t * k + v)
                    dve.wait_ge(chunk_done, step(6, (n if j == 0 else n + 3 * j - 1) + 2))
                    dve.wait_ge(cols_copied, step(2, at.copied + j + 1))
                    up = C[:, 2 * (j % 2) + 1, :]
                    V.tensor_tensor(full[j % 2], up, relu[j % 2], ALU.mult)
                    V.tensor_tensor(hid_h[:, j % 2, :], up, relu[j % 2], ALU.mult).then_inc(up_used, 1)
                    dve.wait_ge(up_used, step(2, at.up + j + 1))
                    V.tensor_tensor(hid_l[:, j % 2, :], full[j % 2], hid_h[:, j % 2, :].bitcast(f32),
                                    ALU.subtract).then_inc(hid_lo, 1)

                lo(n + AHEAD)
                lo(n + 1 + AHEAD)
                units(0)

                def three(j, t=None):
                    b = n + 2 + 3 * j + AHEAD
                    lo(b, t)
                    lo(b + 1, t)
                    units(j + 1, t)
                    lo(b + 2, t)

                turns = glu_turns(n)
                with nc.vector.Fori(0, turns) as t:
                    for j in range(2):
                        three(j, t)
                for j in range(2 * turns, N_GLU - 1):
                    three(j)

            def contexts(i, at, kind):
                dve.wait_ge(ctx_hi, at.ctx + i + 1)
                if kind == "mem":
                    V.tensor_tensor(at_l[:, 2 * i:2 * i + 2, :], tiles(Y[:, i % 2, :], 2),
                                    at_h[:, 2 * i:2 * i + 2, :].bitcast(f32), ALU.subtract).then_inc(ctx_lo, 1)
                else:
                    V.tensor_tensor(at_l[:, i, :], Y[:, i % 2, 0:S], at_h[:, i, :].bitcast(f32),
                                    ALU.subtract).then_inc(ctx_lo, 1)

            def softmax(kind, heads, at):
                h0 = at.head
                rows = rows_of(kind)
                for i in range(heads + 5):
                    if i < heads:
                        two = slice(2 * i, 2 * i + 2)
                        dve.wait_ge(scores_ready, h0 + i + 1)
                        if i >= 2:
                            dve.wait_ge(probs_ready, h0 + i - 1)
                        if kind == "mem":
                            ins = V.reduce_max(a_stat[:, 4, two], tiles(C[:, i % 2, :], 2), X)
                        else:
                            for b, (first, end) in enumerate(rows):
                                ins = V.tensor_tensor_reduce(
                                    out=sc[i % 2][:, first:end], in0=C[:, i % 2, first:end], in1=mask[:, first:end], scale=0.125,
                                    scalar=LOWEST, op0=ALU.add, op1=ALU.max, accum_out=a_stat[:, 4, 2 * i + b:2 * i + b + 1])
                        ins.then_inc(scores_scaled, 1)
                        dve.wait_ge(scores_scaled, h0 + i + 1)
                        if kind == "swa":
                            V.tensor_scalar(a_stat[:, 0, two], a_stat[:, 4, two], -1.0, sinks[:, 16 + i:17 + i], ALU.mult,
                                            ALU.min).then_inc(scores_max, 1)
                        else:
                            V.tensor_scalar(a_stat[:, 0, two], a_stat[:, 4, two], -0.0625 if kind == "mem" else -1.0, None,
                                            ALU.mult).then_inc(scores_max, 1)
                    if 1 <= i <= heads:
                        k = i - 1
                        two = slice(2 * k, 2 * k + 2)
                        dve.wait_ge(probs_ready, h0 + k + 1)
                        if kind == "swa":
                            again(V.tensor_tensor(a_stat[:, 1, two], a_stat[:, 1, two], a_stat[:, 3, two], ALU.add))
                        again(V.reciprocal(a_stat[:, 2, two], a_stat[:, 1, two]))
                        for b, (first, end) in enumerate(rows):
                            p = pr[k % 3][:, first:end]
                            last = V.tensor_scalar(p, p, a_stat[:, 2, 2 * k + b:2 * k + b + 1], None, ALU.mult)
                        last.then_inc(probs_scaled, 1)
                    if i >= 4 and (kind == "mem" or i % 2 == 1) and i - 4 < heads:
                        contexts(i - 4 if kind == "mem" else (i - 4) // 2, at, kind)

            def rope_(t, c, done):
                cos, sin = (rope[:, i:i + 1, :].broadcast_to([P, 2, S]) for i in range(2))
                dve.wait_ge(turned, done + c + 1)
                if c >= 1:
                    dve.wait_ge(rotated, done + c)
                V.tensor_tensor(tiles(rot[0], 2), halves(t, c), cos, ALU.mult)
                again(V.tensor_tensor(tiles(rot[1], 2), tiles(Y[:, c, :], 2), sin, ALU.mult))
                V.tensor_tensor(halves(t, c), tiles(rot[0], 2), tiles(rot[1], 2), ALU.add).then_inc(rotated, 1)

            def rope_keys(at):
                dve.wait_ge(swa_in, 16 * 7)
                V.tensor_scalar(sinks[:, 16:32], sinks[:, 0:16], -1.0, None, ALU.mult).then_inc(sink_ready, 1)
                rope_(kT, 0, at.rot - 1)

            def q_cols_(n, at):
                for i in range(n):
                    lo(at.chunk + i + AHEAD)
                    if i >= 1:
                        rope_(qT, i - 1, at.rot)
                rope_(qT, n - 1, at.rot)
                dve.wait_ge(sink_ready, 1)

            def stick(at):
                for i in range(16 + 6):
                    if 1 <= i <= 16:
                        h = i - 1
                        k = h % 2
                        beta, z = bias[k][:, 0:SEEN], C[:, k, 0:SEEN]
                        dve.wait_ge(soft_ready, h + 1)
                        if h >= 2:
                            dve.wait_ge(suffix_ready, h - 1)
                            dve.wait_ge(suffix_added, h - 1)
                        again(V.scalar_tensor_tensor(beta, z, 0.0, sc[k][:, 0:SEEN], ALU.min, ALU.subtract))
                        V.tensor_tensor(pr[k][:, 0:SEEN], beta, z, ALU.subtract).then_inc(keep_ready, 1)
                    if 2 <= i < 16 + 2:
                        h = i - 2
                        dve.wait_ge(suffix_ready, h + 1)
                        if h >= 3:
                            dve.wait_ge(weights_used, h - 2)
                        V.tensor_tensor(pT[h % 3][:, 0:SEEN], C[:, 2 + h % 2, 0:SEEN], bias[h % 2][:, 0:SEEN],
                                        ALU.add).then_inc(suffix_added, 1)
                    if i >= 6 and i % 2 == 0:
                        contexts((i - 6) // 2, at, "stick")

            def even_cols_(n, at):
                f = f_t.rearrange(flat)
                by_block = lambda t: t[:, None, :].broadcast_to([P, TB, 512])
                for i in range(n):
                    lo(at.chunk + i + AHEAD)
                    if i == 0:
                        dve.wait_ge(lb_in, 16)
                        V.tensor_tensor(lb, lb, lb, ALU.subtract).then_inc(lb_shifted, 1)
                    elif i == 1:
                        norm_scale("mem", at)
                    elif i == 2:
                        dve.wait_ge(lb_exp, 1)
                        again(V.reciprocal(lb, not_lb))
                    elif i == 3:
                        dve.wait_ge(cols_copied, at.copied + 4)
                        V.tensor_scalar(f, f, GATE_CLIP, -GATE_CLIP, ALU.min, ALU.max).then_inc(clipped, 1)
                        again(V.tensor_tensor(not_lb, not_lb, lb, ALU.mult))
                        again(V.tensor_tensor(lb, not_lb, not_lb, ALU.subtract))
                        again(V.tensor_scalar(lb, lb, 0.0, 1.0, ALU.max, ALU.min))
                        again(V.tensor_scalar(not_lb, lb, -1.0, 1.0, ALU.mult, ALU.add))
                    elif i == 4:
                        norm_lo("mem", at, Y)
                    elif i == 5:
                        dve.wait_ge(even_in, 16 * 7)
                        by_head = g_t.rearrange("p b (h d) -> p (b h) d", h=4)
                        V.tensor_tensor(by_head, by_head, og[:, None, :].broadcast_to([P, 8, P]), ALU.mult).then_inc(gated, 1)
                    elif i == 6:
                        dve.wait_ge(gates_exp, 1)
                        again(V.scalar_tensor_tensor(soft_f, f, 0.0, soft_f, ALU.min, ALU.subtract))
                        V.tensor_tensor(key, soft_f, f, ALU.subtract).then_inc(keys_shared, 1)
                    elif i == 7:
                        V.tensor_tensor(tiles(xn[:, 0, :], 2), tiles(exp_f, 2), by_block(lb), ALU.mult).then_inc(lb_scaled, 1)
                        dve.wait_ge(keys_exp, 1)
                        V.tensor_tensor(tiles(key, 2), tiles(key, 2), by_block(not_lb), ALU.mult).then_inc(keys_ready, 1)
                    elif i == 8:
                        dve.wait_ge(gates_ln, 1)
                        dve.wait_ge(keys_shared, 1)
                        V.tensor_tensor(f, soft_f, xn[:, 0, :], ALU.add).then_inc(decays_ready, 1)

            def even(at):
                dve.wait_ge(mix_hi, 1)
                for g in range(4):
                    last = V.scalar_tensor_tensor(at_l[:, g, :], Y[:, 2 + g // 2, g % 2 * S:(g % 2 + 1) * S], pscale[:, g:g + 1],
                                                  at_h[:, g, :].bitcast(f32), ALU.mult, ALU.subtract)
                last.then_inc(mix_lo, 1)
                dve.wait_ge(level_score, 1)
                for b in range(TB):
                    dve.wait_ge(ident_in, 16)
                    last = V.tensor_tensor(score[b], tiles(C[:, b, :], 4), ident[:, None, :].broadcast_to([P, 4, P]), ALU.mult)
                last.then_inc(level_used, 1)
                for l in range(2 + len(LEVELS)):
                    if l < 1 + len(LEVELS):
                        dve.wait_ge(level_exp, l + 1)
                        if l >= 2:
                            dve.wait_ge(level_score, l)
                        m = P if l == 0 else LEVELS[l - 1]
                        by_half = lambda t, k: t.rearrange(flat).rearrange("p (j two m) -> p j two m", two=2, m=m)[:, :, k, :]
                        decay = tiles(fall[l % 2], 4)
                        V.tensor_tensor(by_half(both[l % 2], 0), by_half(k_d, 0), by_half(decay, 0), ALU.mult)
                        V.tensor_tensor(by_half(both[l % 2], 1), by_half(q_d, 1), by_half(decay, 1), ALU.mult).then_inc(level_both, 1)
                    if l >= 1:
                        dve.wait_ge(level_score, l + 1)
                        bank = 2 * (l % 2)
                        if l == 1:
                            V.tensor_copy(score[2], tiles(C[:, bank, :], 4)).then_inc(level_used, 1)
                        else:
                            pairs = pair_c[:, (l - 2) * P:(l - 1) * P].bitcast(i32)[:, None, :].broadcast_to([P, 4, P])
                            dve.wait_ge(level_used, l)
                            for b in range(TB):
                                last = V.copy_predicated(score[b], pairs, tiles(C[:, bank + b, :], 4))
                            last.then_inc(level_used, 1)
                dve.wait_ge(rec_squared, 1)
                for b in range(TB):
                    last = V.reduce_sum(h_stat[:, 0, 4 * b:4 * b + 4], tiles(xn[:, b, 512:1024], 4), X)
                last.then_inc(rec_meaned, 1)
                dve.wait_ge(rec_guessed, 1)
                again(V.tensor_scalar(h_stat[:, 3, :], h_stat[:, 0, :], 1.0 / P, EPS, ALU.mult, ALU.add))
                newton(h_stat[:, 2, :], h_stat[:, 3, :], [h_stat[:, k, :] for k in range(4, 7)])
                for b in range(TB):
                    r = h_stat[:, 6, 4 * b:4 * b + 4][:, :, None].broadcast_to([P, 4, P])
                    again(V.tensor_tensor(tiles(xn[:, b, 0:512], 4), tiles(C[:, 2 + b, :], 4), r, ALU.mult))
                    V.tensor_tensor(xn[:, b, 0:512], xn[:, b, 0:512], g_t[:, b, :], ALU.mult).then_inc(rec_normed, 1)
                lo(at.chunk + AHEAD)
                for b in range(TB):
                    dve.wait_ge(rec_hi, b + 1)
                    part = (slice(None), slice(4, 8), slice(b * P, (b + 1) * P))
                    V.tensor_tensor(at_l[part], tiles(C[:, b, :], 4), at_h[part].bitcast(f32), ALU.subtract).then_inc(rec_lo, 1)
                lo(at.chunk + 1 + AHEAD)

            for s, at in before:
                if s[0] == "norm":
                    norm(s[1], at)
                elif s[0] == "post":
                    post(at)
                elif s[0] == "add":
                    add(s[1], at)
                elif s[0] == "meanwhile":
                    meanwhile(len(s[1]), at)
                elif s[0] in ("cols", "kv_cols"):
                    cols(0, len(s[1]), at)
                elif s[0] == "even_cols":
                    even_cols_(len(s[1]), at)
                elif s[0] == "rows":
                    cols(2 if s[1] == "w_out_ab" else 0, 3, at)
                elif s[0] == "relu_ff":
                    relu_ff(at)
                elif s[0] == "swiglu":
                    swiglu(at)
                elif s[0] == "softmax":
                    softmax(s[1], s[2], at)
                elif s[0] == "q_cols":
                    q_cols_(len(s[1]), at)
                elif s[0] == "stick":
                    stick(at)
                elif s[0] == "even":
                    even(at)

        @block.tensor
        def _(pe):
            mm = nc.tensor.matmul

            def split_ready(n, t=None):
                pe.wait_ge(lo_split, n + 1 if t is None else t * 6 + (n + 1))

            def col_chunk(n, kind, h, l, bank, t=None, split=None):
                split_ready(n, t)
                if split is not None:
                    pe.wait_ge(at_lo, split + 1)
                wh, wl = (w[:, n % RING, :].rearrange("p (k c) -> p k c", k=KT) for w in (w_hi, w_lo))
                for i in range(2):
                    part = slice(i * P, (i + 1) * P)
                    to = C[:, bank, i * S:(i + 1) * S]
                    if kind == "T":
                        passes = [((wh[:, k, part], h[:, k, :]), (wh[:, k, part], l[:, k, :]), (wl[:, k, part], h[:, k, :]))
                                  for k in range(KT)]
                    else:
                        passes = [((h[:, k, part], wh[:, k, :]), (h[:, k, part], wl[:, k, :]), (l[:, k, part], wh[:, k, :]))
                                  for k in range(KT)]
                    order = [(k, j) for k in range(KT) for j in range(3)]
                    if split is not None:
                        order = [(k, j) for j in ((0, 2, 1) if kind == "T" else (0, 1, 2)) for k in range(KT)]
                    for step, (k, j) in enumerate(order):
                        if split is not None and step % 4 == 0 and (kind == "N" or i == 0) and step // KT != 1:
                            pe.wait_ge(at_hi if step < KT else at_lo, split + (2 * i if kind == "N" else 2) + k // 4 + 1)
                        last = mm(to, *passes[k][j], start=step == 0, stop=step == 3 * KT - 1)
                last.then_inc(chunk_done, 1)

            def row_chunk(n, h, l, first, end, t=None):
                split_ready(n, t)
                wh, wl = (w[:, n % RING, :].rearrange("p (k c) -> p k c", k=2) for w in (w_hi, w_lo))
                for b in range(TB):
                    for k in range(2):
                        part = slice(b * P, (b + 1) * P)
                        for still, moving, j in ((h[k], wh, 0), (h[k], wl, 1), (l[k], wh, 2)):
                            for half in range(2):
                                last = mm(Y[:, 2 * b + half, :], still[:, part], moving[:, k, half * 512:(half + 1) * 512],
                                          start=first and k == 0 and j == 0, stop=end and k == 1 and j == 2)
                    if b == 1:
                        last.then_inc(chunk_done, 1)
                    elif end:
                        last.then_inc(y_ready, 1)

            def cols(specs, at, some=None):
                for i in range(len(specs)) if some is None else some:
                    kind, src = specs[i][3:]
                    if i >= 4:
                        pe.wait_ge(cols_copied, at.copied + i - 3)
                    h, l = (mem_h, mem_l) if src == "mem" else (at_h, at_l)
                    col_chunk(at.chunk + i, kind, h, l, i % 4, split=at.turned - 4 if src == "at" and i == 0 else None)

            def meanwhile(specs, at):
                n = len(specs)
                pe.wait_ge(cols_copied, at.copied)
                cols(specs, at, range(n - 1))
                norm(behind_post(at), Y)
                cols(specs, at, range(n - 1, n))

            def rows(at, some):
                for r in some:
                    row_chunk(at.chunk + r, [at_h[:, 2 * r + k, :] for k in range(2)], [at_l[:, 2 * r + k, :] for k in range(2)],
                                     r == 0, r == 3)

            def norm(at, banks, doubled=False, warm=False):
                for b in range(TB):
                    if doubled and b == 1:
                        pe.wait_ge(kdup_copied, 1)
                    elif warm and b == 1:
                        stay_warm(WARM_BLOCK)
                    pe.wait_ge(xn_ready, at.xn + b + 1)
                    for h in range(2):
                        for k in range(4):
                            last = nc.tensor.transpose(banks[:, 2 * b + h, k * P:(k + 1) * P],
                                                       xn[:, b, (4 * h + k) * P:(4 * h + k + 1) * P], ident[:])
                        last.then_inc(xt_ready, 1)

            def stay_warm(n):
                for _ in range(n):
                    mm(C[:, 3, :], zeros[:, 0:P], zeros[:], start=True, stop=True)

            def clear_y(at):
                pe.wait_ge(x_ready, at.x)
                if at.rot > 0:
                    pe.wait_ge(rotated, at.rot)
                for i in range(4):
                    mm(Y[:, i, :], zeros[:, 0:P], zeros[:], start=True, stop=False)

            def hidden(slot):
                return [[t[:, slot, k * S:(k + 1) * S] for k in range(2)] for t in (hid_h, hid_l)]

            def relu_ff(at):
                n = at.chunk

                def up(j, t=None):
                    col_chunk(n + 2 * j - 1, "T", at_h, at_l, j % 3, t)

                def down(j, t=None, end=False):
                    pe.wait_ge(hid_lo, at.hid + j + 1 if t is None else t * 3 + (at.hid + j + 1))
                    row_chunk(n + 2 * N_REL - 1 if end else n + 2 * j + 2, *hidden(j % 3), False, end, t)

                col_chunk(n, "T", at_h, at_l, 0, split=at.turned - 4)
                with nc.tensor.Fori(0, (N_REL - 1) // 3) as t:
                    for j in range(3):
                        up(j + 1, t)
                        down(j, t)
                down(N_REL - 1, end=True)

            def swiglu(at, same):
                n = at.chunk

                def gate_up(j, t=None):
                    col_chunk(n + 3 * j - 1, "T", at_h, at_l, 2 * (j % 2), t)
                    col_chunk(n + 3 * j, "T", at_h, at_l, 2 * (j % 2) + 1, t)

                def down(j, t=None, end=False):
                    pe.wait_ge(hid_lo, at.hid + j + 1 if t is None else t * 2 + (at.hid + j + 1))
                    row_chunk(n + 3 * N_GLU - 1 if end else n + 3 * j + 4, *hidden(j % 2), False, end, t)

                col_chunk(n, "T", at_h, at_l, 0, split=at.turned - 4)
                if same:
                    clear_y(at)
                col_chunk(n + 1, "T", at_h, at_l, 1)
                with nc.tensor.Fori(0, (N_GLU - 1) // 2) as t:
                    for j in range(2):
                        gate_up(j + 1, t)
                        down(j, t)
                down(N_GLU - 1, end=True)

            def half_of(t, h):
                return t[64 * (h % 2):64 * (h % 2) + 64, h // 2, :]

            def context(i, values, weights, used):
                rows, bank = slice(64 * (i % 2), 64 * (i % 2) + 64), (i // 2) % 2
                mm(Y[rows, bank, 0:S], values(0), weights[:, 0:S], start=True, stop=False)
                mm(Y[rows, bank, P:S], values(1), weights[:, S:SEEN], start=False, stop=True).then_inc(used, 1)

            def softmax(kind, heads, at):
                h0 = at.head
                pe.wait_ge(cols_copied, at.copied)
                if kind == "band":
                    pe.wait_ge(band_in, 32)
                for i in range(heads + 3):
                    if i < heads:
                        if i >= 2:
                            pe.wait_ge(probs_ready if kind == "mem" else scores_scaled, h0 + i - 1)
                        if kind == "swa" and i % 4 == 0:
                            pe.wait_ge(rotated, at.rot - 3 + i // 4)
                        if kind == "band" and i % 2 == 0:
                            pe.wait_ge(bias_in[i // 2 % 2], 16 * (i // 4 + 1))
                        for b, (first, end) in enumerate(rows_of(kind)):
                            q, keys = slice(b * P, (b + 1) * P), slice(0, end - first)
                            to = C[:, i % 2, first:end]
                            if kind == "mem":
                                for k in range(2):
                                    last = mm(to, qT[:, 2 * i + k, q], mem_kT[:, 2 * i + k, :], start=k == 0, stop=k == 1)
                            elif kind == "band":
                                mm(to, half_of(qT, i)[:, q], half_of(kT, i)[:, keys], start=True, stop=False)
                                some = bias[i // 2 % 2][:, i % 2 * S + (1 - b) * P:i % 2 * S + S]
                                last = mm(to, flip_c, some, start=False, stop=True)
                            else:
                                part = slice(64 * (i % 2), 64 * (i % 2) + 64)
                                last = mm(to, half_of(qT, i)[:, q], kdup[part, i // 4, keys], start=True, stop=True)
                        last.then_inc(scores_ready, 1)
                    if 2 <= i < heads + 2:
                        k = i - 2
                        pe.wait_ge(probs_scaled, h0 + k + 1)
                        if k >= 2:
                            pe.wait_ge(probs_copied, h0 + k - 1)
                        turn = ((0, 0), (1, 2), (2, 1), (3, 3)) if kind == "mem" else ((0, 0), (1, 1), (2, 2))
                        for to, src in turn:
                            last = nc.tensor.transpose(C[:, 2 + k % 2, to * P:(to + 1) * P], pr[k % 3][:, src * P:(src + 1) * P], ident[:])
                        last.then_inc(probs_turned, 1)
                    if i >= 3:
                        k = i - 3
                        pe.wait_ge(probs_copied, h0 + k + 1)
                        if kind == "mem":
                            if k >= 2:
                                pe.wait_ge(ctx_lo, at.ctx + k - 1)
                            for half in range(2):
                                for kb in range(2):
                                    first = k * S + half * P
                                    last = mm(Y[:, k % 2, half * S:(half + 1) * S], vt[:, kb, first:first + P],
                                              pT[k % 2][:, kb * S:(kb + 1) * S], start=kb == 0, stop=kb == 1)
                            last.then_inc(probs_used, 1)
                        else:
                            if k >= 4 and k % 2 == 0:
                                pe.wait_ge(ctx_lo, at.ctx + k // 2 - 1)
                            head = k if kind == "band" else k // 4
                            context(k, lambda kb: vt[:, kb, head * 64:head * 64 + 64], pT[k % 2], probs_used)
                pe.wait_ge(ctx_lo, at.ctx + (4 if kind == "mem" else 8))

            def rope_(t, c, at):
                mm(Y[:, c, :], turn_c, halves(t, c), start=True, stop=True).then_inc(turned, 1)

            def rope_keys(at):
                pe.wait_ge(cols_copied, at.copied + 2)
                pe.wait_ge(swa_in, 16 * 7)
                rope_(kT, 0, at)

            def q_cols_(specs, at):
                n = len(specs)
                for i in range(n + 1):
                    if i < n:
                        cols(specs, at, [i])
                    if i >= 1:
                        pe.wait_ge(cols_copied, at.copied + i)
                        rope_(qT, i - 1, at)

            def double(at):
                pe.wait_ge(rotated, at.rot)
                for h in range(4):
                    last = mm(C[:, 2 + h // 2, h % 2 * S:(h % 2 + 1) * S], low_c if h % 2 == 0 else high_c, kT[:, h // 2, :],
                              start=True, stop=True)
                last.then_inc(kdup_ready, 1)

            def stick(at):
                pe.wait_ge(cols_copied, at.copied)
                pe.wait_ge(stick_in, 48)
                for i in range(16 + 4):
                    if i < 16:
                        if i >= 2:
                            pe.wait_ge(keep_ready, i - 1)
                        mm(C[:, i % 2, 0:S], half_of(kT, i)[:, 0:P], half_of(qT, i), start=True, stop=True)
                        mm(C[:, i % 2, S:SEEN], half_of(kT, i)[:, P:S], half_of(qT, i)[:, P:S], start=True,
                           stop=True).then_inc(z_ready, 1)
                    if 2 <= i < 16 + 2:
                        h = i - 2
                        keep, bank = pr[h % 2], 2 + h % 2
                        pe.wait_ge(keep_masked, h + 1)
                        if h >= 2:
                            pe.wait_ge(suffix_added, h - 1)
                        mm(C[:, bank, 0:S], after_s, keep[:, 0:S], start=True, stop=False)
                        mm(C[:, bank, P:S], ones_s, keep[:, S:SEEN], start=False, stop=True)
                        mm(C[:, bank, S:SEEN], after_s, keep[:, S:SEEN], start=True, stop=True).then_inc(suffix_ready, 1)
                    if i >= 4:
                        h = i - 4
                        pe.wait_ge(weights_masked, h + 1)
                        if h >= 4 and h % 2 == 0:
                            pe.wait_ge(ctx_lo, at.ctx + h // 2 - 1)
                        context(h, lambda kb: vt[:, kb, h * 64:h * 64 + 64], pT[h % 3], weights_used)
                pe.wait_ge(ctx_lo, at.ctx + 8)

            def even_cols_(specs, at):
                for i in range(len(specs)):
                    cols(specs, at, [i])
                    if i == 3:
                        norm(at, Y)
                    elif i == 6:
                        pe.wait_ge(at_lo, at.turned + 4)
                        pe.wait_ge(pool_in, 32)
                        pe.wait_ge(cols_copied, at.copied + 6)
                        for g in range(4):
                            for b in range(TB):
                                table = pool_c[g // 2][:, (g % 2 * 2 + b) * S:(g % 2 * 2 + b + 1) * S]
                                last = mm(Y[:, 2 + g // 2, g % 2 * S:(g % 2 + 1) * S], u_t[:, b, g * P:(g + 1) * P], table,
                                          start=b == 0, stop=b == 1)
                        last.then_inc(pool_ready, 1)
                    elif i == 8:
                        pe.wait_ge(keys_ready, 1)
                        for b in range(TB):
                            for h in range(4):
                                last = nc.tensor.transpose(Y[:, b, h * P:(h + 1) * P], tiles(key, 8)[:, 4 * b + h, :], ident[:])
                        last.then_inc(keys_turned, 1)
                        pe.wait_ge(pool_copied, 1)
                        pe.wait_ge(even_in, 16 * 7)
                        for g in range(4):
                            last = mm(Y[:, 2 + g // 2, g % 2 * S:(g % 2 + 1) * S], pool_w[:, g, :], pooled[:, g, :],
                                      start=True, stop=True)
                        last.then_inc(mix_ready, 1)

            def even(at):
                pe.wait_ge(decays_ready, 1)
                pe.wait_ge(keys_copied, 1)
                for l in range(2 + len(LEVELS)):
                    if l < 1 + len(LEVELS):
                        if l == 1:
                            pe.wait_ge(mix_lo, 1)
                        if l >= 2:
                            pe.wait_ge(level_exp, l - 1)
                        for h in range(4):
                            for b in range(TB):
                                table = (after_c, upto_c)[b] if l == 0 else span_c[:, (l - 1) * P:l * P]
                                to = h % 2 * S + b * P
                                last = mm(Y[:, 2 * (l % 2) + h // 2, to:to + P], f_t[:, b, h * P:(h + 1) * P], table,
                                          start=True, stop=True)
                        last.then_inc(level_sum, 1)
                    if l == 0:
                        pe.wait_ge(cols_copied, at.copied)
                        for b in range(TB):
                            part = slice(b * P, (b + 1) * P)
                            for h in range(4):
                                last = mm(C[:, b, h * P:(h + 1) * P], k_d[:, h, part], q_d[:, h, part], start=True, stop=True)
                        last.then_inc(level_score, 1)
                    if l >= 1:
                        pe.wait_ge(level_both, l)
                        pe.wait_ge(level_used, l - 1 if l >= 2 else 1)
                        qk = both[(l - 1) % 2]
                        bank = 2 * (l % 2)
                        for b in range(1 if l == 1 else TB):
                            for h in range(4):
                                keys = qk[:, h, 0:P] if l == 1 else qk[:, h, b * P:(b + 1) * P]
                                queries = qk[:, h, P:S] if l == 1 else keys
                                last = mm(C[:, bank + b, h * P:(h + 1) * P], keys, queries, start=True, stop=True)
                        last.then_inc(level_score, 1)
                pe.wait_ge(level_used, 2 + len(LEVELS))
                pe.wait_ge(level_exp, 1 + len(LEVELS))
                for b in range(TB):
                    for h in range(4):
                        head = slice(h * P, (h + 1) * P)
                        if b == 1:
                            mm(C[:, 2 + b, head], score[2][:, h, :], v_t[:, 0, head], start=True, stop=False)
                        last = mm(C[:, 2 + b, head], score[b][:, h, :], v_t[:, b, head], start=b == 0, stop=True)
                last.then_inc(rec_ready, 1)
                rows(at, range(2))
                for b in range(TB):
                    pe.wait_ge(rec_normed, b + 1)
                    for h in range(4):
                        last = nc.tensor.transpose(C[:, b, h * P:(h + 1) * P], xn[:, b, h * P:(h + 1) * P], ident[:])
                    last.then_inc(rec_turned, 1)
                pe.wait_ge(rec_lo, TB)

            pe.wait_ge(ident_in, 16)
            pe.wait_ge(setup, 1)
            for (s, at), last, after in zip(before, [None] + net, net[1:] + [None]):
                if s[0] == "norm" and s[1] != "out":
                    if last is None:
                        stay_warm(WARM_START)
                    elif last[0] == "post":
                        stay_warm(WARM_POST)
                    elif last[0] == "add":
                        stay_warm(WARM_ADD)
                    if after[0] in ("relu_ff", "swiglu") and s[1] != "same":
                        clear_y(at)
                    if s[1] == "same":
                        pe.wait_ge(cols_copied, at.copied)
                    if len(s) > 2:
                        double(at)
                    norm(at, C, len(s) > 2, s[1] == "at")
                elif s[0] == "meanwhile":
                    meanwhile(s[1], at)
                elif s[0] == "cols":
                    cols(s[1], at)
                elif s[0] == "rows":
                    rows(at, range(2 if s[1] == "w_out_ab" else 0, 4))
                elif s[0] == "even_cols":
                    even_cols_(s[1], at)
                elif s[0] == "relu_ff":
                    relu_ff(at)
                elif s[0] == "swiglu":
                    swiglu(at, last == ("norm", "same"))
                elif s[0] == "softmax":
                    softmax(s[1], s[2], at)
                elif s[0] == "kv_cols":
                    cols(s[1], at)
                    rope_keys(at)
                elif s[0] == "q_cols":
                    q_cols_(s[1], at)
                elif s[0] == "stick":
                    stick(at)
                elif s[0] == "even":
                    even(at)


def kernel(**inputs):
    import concourse.bacc as bacc
    from concourse.bass_utils import run_bass_kernel_spmd

    nc = bacc.Bacc("TRN2", target_bir_lowering=False, num_devices=1)
    arrays, args = {}, {}
    data = {k: np.ascontiguousarray(v) for k, v in inputs.items() if k not in ("rel_bias", "pool_scale")}
    data["pool_scale_by_group"] = np.ascontiguousarray(np.asarray(inputs["pool_scale"]).reshape(4, P).T)
    data["rel_reversed"] = np.ascontiguousarray(np.asarray(inputs["rel_bias"])[0, :, ::-1])
    data.update(constants())
    for name, v in data.items():
        arrays["in_" + name] = v
        args[name] = nc.dram_tensor("in_" + name, v.shape, mybir.dt.from_np(v.dtype), kind="ExternalInput").ap()
    out = nc.dram_tensor("out_0", (1, S, D), mybir.dt.float32, kind="ExternalOutput").ap()
    build(nc, args, out)
    r = run_bass_kernel_spmd(nc, [arrays], core_ids=[0])
    return r.results[0]["out_0"]
```
